# Optimizing a Trainium2 kernel written in Bass

```python
import jax, jax.numpy as jnp
from jax import lax
import numpy as np

D_MODEL = 1024
BATCH = 1
SEQ = 256
DEPTH = 1

CHUNK = 64
WINDOW = 128
WINDOW_CHUNKS = WINDOW // CHUNK
HEAD_DIM = 64
N_Q_HEADS = D_MODEL // HEAD_DIM
N_KV_HEADS = 2
GQA_GROUP = N_Q_HEADS // N_KV_HEADS
ATTN_DIM = N_Q_HEADS * HEAD_DIM
KV_DIM = N_KV_HEADS * HEAD_DIM
POOL_WINDOWS = (2, 4, 8, 16)
N_POOL_GROUPS = len(POOL_WINDOWS)
POOL_DIM = D_MODEL // 2
POOL_GROUP_DIM = POOL_DIM // N_POOL_GROUPS
SPLITS = [ATTN_DIM, ATTN_DIM + KV_DIM, ATTN_DIM + 2 * KV_DIM,
          ATTN_DIM + 2 * KV_DIM + POOL_DIM, ATTN_DIM + 2 * KV_DIM + POOL_DIM + D_MODEL]
IN_DIM = ATTN_DIM + 2 * KV_DIM + POOL_DIM + 2 * D_MODEL
N_EXPERTS = 32
TOP_K = 4
D_FF = D_MODEL
SWIGLU_ALPHA = 1.702
SWIGLU_LIMIT = 7.0
MOE_BLOCK = 256
LN_EPS = 1e-5
DEEPNORM_ALPHA = (2 * DEPTH) ** 0.25
DEEPNORM_BETA = (8 * DEPTH) ** -0.25
NEG_INF = -1e30

kernel_name = "hybrid_swa_sink_pool_moe_deepnorm"

def layer_norm(x, g, b):
    xf = x.astype(jnp.float32)
    mu = jnp.mean(xf, axis=-1, keepdims=True)
    var = jnp.mean(jnp.square(xf - mu), axis=-1, keepdims=True)
    y = (xf - mu) * lax.rsqrt(var + LN_EPS) * g.astype(jnp.float32) + b.astype(jnp.float32)
    return y.astype(x.dtype)

def sliding_window_sink_attention(q, k, v, sinks):
    B, S = q.shape[0], q.shape[1]
    nc = S // CHUNK
    qc = q.reshape(B, nc, CHUNK, N_KV_HEADS, GQA_GROUP, HEAD_DIM)

    def band(t):
        t = t.reshape(B, nc, CHUNK, N_KV_HEADS, HEAD_DIM)
        t = jnp.pad(t, ((0, 0), (WINDOW_CHUNKS - 1, 0), (0, 0), (0, 0), (0, 0)))
        return jnp.concatenate([t[:, i:i + nc] for i in range(WINDOW_CHUNKS)], axis=2)

    kb, vb = band(k), band(v)
    scores = jnp.einsum('bnqhgd,bnkhd->bnhgqk', qc, kb,
                        preferred_element_type=jnp.float32) * (HEAD_DIM ** -0.5)
    key_chunk = (jnp.arange(nc)[:, None] - (WINDOW_CHUNKS - 1)
                 + jnp.arange(WINDOW_CHUNKS * CHUNK)[None, :] // CHUNK)
    valid = key_chunk >= 0
    scores = jnp.where(valid[None, :, None, None, None, :], scores, NEG_INF)
    sink = sinks.astype(jnp.float32).reshape(N_KV_HEADS, GQA_GROUP)[None, None, :, :, None, None]
    m = jnp.maximum(jnp.max(scores, axis=-1, keepdims=True), sink)
    p = jnp.exp(scores - m)
    denom = jnp.sum(p, axis=-1, keepdims=True) + jnp.exp(sink - m)
    probs = (p / denom).astype(v.dtype)
    o = jnp.einsum('bnhgqk,bnkhd->bnqhgd', probs, vb)
    return o.reshape(B, S, ATTN_DIM)

def multiscale_pool(u, w_mix, scale):
    B, S = u.shape[0], u.shape[1]
    uf = u.astype(jnp.float32).reshape(B, S, N_POOL_GROUPS, POOL_GROUP_DIM)
    pos1 = jnp.arange(1, S + 1)
    outs = []
    for g, w in enumerate(POOL_WINDOWS):
        ug = uf[:, :, g]
        csum = jnp.concatenate([jnp.zeros((B, w, POOL_GROUP_DIM), jnp.float32),
                                jnp.cumsum(ug, axis=1)], axis=1)
        window_sum = csum[:, w:] - csum[:, :S]
        count = jnp.minimum(pos1, w).astype(jnp.float32)[None, :, None]
        outs.append(window_sum / count - ug)
    r = jnp.stack(outs, axis=2).astype(u.dtype)
    y = jnp.einsum('bsgc,gcd->bsgd', r, w_mix).reshape(B, S, POOL_DIM)
    return y * scale

def hybrid_mixer(x, w_in, b_in, sinks, w_o_attn, w_pool_mix, pool_scale, w_o_pool, w_out):
    B, S, _ = x.shape
    proj = x @ w_in + b_in
    q, k, v, u, g_attn, g_pool = jnp.split(proj, SPLITS, axis=-1)
    q = q.reshape(B, S, N_Q_HEADS, HEAD_DIM)
    k = k.reshape(B, S, N_KV_HEADS, HEAD_DIM)
    v = v.reshape(B, S, N_KV_HEADS, HEAD_DIM)
    y_attn = sliding_window_sink_attention(q, k, v, sinks) @ w_o_attn
    y_pool = multiscale_pool(u, w_pool_mix, pool_scale) @ w_o_pool
    merged = jax.nn.sigmoid(g_attn) * y_attn + jax.nn.sigmoid(g_pool) * y_pool
    return merged @ w_out

def topk_moe(h, w_router, b_router, w_gu, b_gu, w_down, b_down):
    B, S, D = h.shape
    T = B * S
    n_assign = T * TOP_K
    n_blocks = -(-n_assign // MOE_BLOCK) + N_EXPERTS
    ht = h.reshape(T, D)
    logits = (ht @ w_router + b_router).astype(jnp.float32)
    top_v, top_e = lax.top_k(logits, TOP_K)
    gates = jax.nn.softmax(top_v, axis=-1)
    flat_e = top_e.reshape(-1)
    order = jnp.argsort(flat_e)
    sorted_e = flat_e[order]
    counts = jnp.bincount(flat_e, length=N_EXPERTS)
    padded = ((counts + MOE_BLOCK - 1) // MOE_BLOCK) * MOE_BLOCK
    pad_end = jnp.cumsum(padded)
    pad_start = pad_end - padded
    start = jnp.cumsum(counts) - counts
    rank = jnp.arange(n_assign) - start[sorted_e]
    dest = pad_start[sorted_e] + rank
    slot_tok = jnp.full((n_blocks * MOE_BLOCK,), T, jnp.int32).at[dest].set(
        (order // TOP_K).astype(jnp.int32))
    slot_gate = jnp.zeros((n_blocks * MOE_BLOCK,), jnp.float32).at[dest].set(
        gates.reshape(-1)[order])
    block_expert = jnp.minimum(
        jnp.searchsorted(pad_end // MOE_BLOCK, jnp.arange(n_blocks), side='right'),
        N_EXPERTS - 1).astype(jnp.int32)
    ht_pad = jnp.concatenate([ht, jnp.zeros((1, D), ht.dtype)], axis=0)

    def expert_block(args):
        e, tok = args
        xb = ht_pad[tok]
        gu = xb @ w_gu[e] + b_gu[e]
        gate = jnp.minimum(gu[:, :D_FF], SWIGLU_LIMIT)
        up = jnp.clip(gu[:, D_FF:], -SWIGLU_LIMIT, SWIGLU_LIMIT)
        act = (up + 1) * (gate * jax.nn.sigmoid(SWIGLU_ALPHA * gate))
        return act @ w_down[e] + b_down[e]

    ys = lax.map(expert_block, (block_expert, slot_tok.reshape(n_blocks, MOE_BLOCK)))
    ys = ys.reshape(-1, D).astype(jnp.float32) * slot_gate[:, None]
    out = jax.ops.segment_sum(ys, slot_tok, num_segments=T + 1)[:T]
    return out.astype(h.dtype).reshape(B, S, D)

def setup_inputs(seed: int = 0) -> dict:
    key = jax.random.key(seed)
    ks = jax.random.split(key, 20)
    L, D = DEPTH, D_MODEL
    nrm = lambda k, shape, s: jax.random.normal(k, shape, jnp.float32) * s
    return {
        "x": nrm(ks[0], (BATCH, SEQ, D), 1.0),
        "w_in": nrm(ks[1], (L, D, IN_DIM), D ** -0.5),
        "b_in": nrm(ks[2], (L, IN_DIM), 0.01),
        "sinks": nrm(ks[3], (L, N_Q_HEADS), 0.5),
        "w_o_attn": nrm(ks[4], (L, ATTN_DIM, D), ATTN_DIM ** -0.5),
        "w_pool_mix": nrm(ks[5], (L, N_POOL_GROUPS, POOL_GROUP_DIM, POOL_GROUP_DIM), POOL_GROUP_DIM ** -0.5),
        "pool_scale": 1.0 + nrm(ks[6], (L, POOL_DIM), 0.02),
        "w_o_pool": nrm(ks[7], (L, POOL_DIM, D), POOL_DIM ** -0.5),
        "w_out": nrm(ks[8], (L, D, D), DEEPNORM_BETA * D ** -0.5),
        "ln1_g": 1.0 + nrm(ks[9], (L, D), 0.02),
        "ln1_b": nrm(ks[10], (L, D), 0.02),
        "w_router": nrm(ks[11], (L, D, N_EXPERTS), D ** -0.5),
        "b_router": nrm(ks[12], (L, N_EXPERTS), 0.01),
        "w_gu": nrm(ks[13], (L, N_EXPERTS, D, 2 * D_FF), D ** -0.5),
        "b_gu": nrm(ks[14], (L, N_EXPERTS, 2 * D_FF), 0.01),
        "w_down": nrm(ks[15], (L, N_EXPERTS, D_FF, D), DEEPNORM_BETA * D_FF ** -0.5),
        "b_down": nrm(ks[16], (L, N_EXPERTS, D), 0.01),
        "ln2_g": 1.0 + nrm(ks[17], (L, D), 0.02),
        "ln2_b": nrm(ks[18], (L, D), 0.02),
    }

def reference(x, w_in, b_in, sinks, w_o_attn, w_pool_mix, pool_scale, w_o_pool, w_out,
              ln1_g, ln1_b, w_router, b_router, w_gu, b_gu, w_down, b_down, ln2_g, ln2_b):
    for l in range(DEPTH):
        h = hybrid_mixer(x, w_in[l], b_in[l], sinks[l], w_o_attn[l], w_pool_mix[l],
                         pool_scale[l], w_o_pool[l], w_out[l])
        x = layer_norm(DEEPNORM_ALPHA * x + h, ln1_g[l], ln1_b[l])
        h = topk_moe(x, w_router[l], b_router[l], w_gu[l], b_gu[l], w_down[l], b_down[l])
        x = layer_norm(DEEPNORM_ALPHA * x + h, ln2_g[l], ln2_b[l])
    return x


_drawn_inputs = setup_inputs


def setup_inputs(seed=0):
    import zlib

    import numpy as np

    out = dict(_drawn_inputs(seed))
    spreads = {}
    factors = {'b_in': 8.0,
     'sinks': 8.0,
     'pool_scale': 4.711,
     'b_router': 3.417,
     'b_gu': 8.0,
     'b_down': 8.0,
     'ln2_g': 2.872,
     'ln2_b': 2.903}
    for name, (base, spread) in spreads.items():
        noise = np.random.default_rng([zlib.crc32(name.encode()), seed]).standard_normal(out[name].shape)
        drawn = base * np.exp(spread * noise) if base else spread * noise
        out[name] = __import__('jax').numpy.asarray(drawn.astype(out[name].dtype))
    for name, factor in factors.items():
        out[name] = (out[name] * factor).astype(out[name].dtype)
    return out
```

```python
from contextlib import ExitStack

import concourse.bass as bass
from concourse import mybir

F32 = mybir.dt.float32
BF16 = mybir.dt.bfloat16
I32 = mybir.dt.int32
U32 = mybir.dt.uint32
ALU = mybir.AluOpType
ACT = mybir.ActivationFunctionType
AX = mybir.AxisListType

P = 128
D = 1024
SEQ = 256
NT = SEQ // P
KD = D // P
CH = 64
HD = 64
NH = D // HD
NKV = 2
NG = 4
PAD = 16
NE = 32
TOPK = 4
F = D
CAP = 64
ROUNDS = SEQ // CAP
SLOTS = 12
GU_CHUNKS = KD
DN_CHUNKS = KD // 2
SLOT = 2 * D
ALPHA = 2 ** 0.25
EPS = 1e-5
NEG = -1e30
SW_ALPHA = 1.702
SW_LIMIT = 7.0
KV0 = D
U0 = KV0 + 2 * NKV * HD
GA0 = U0 + NG * P
GP0 = GA0 + D

TURNS = (["x0", "x1", "x2", "x3", "rows", "k", "v", "q0", "q1", "q2", "q3", "u0", "u1", "ga0"]
         + ["ga1", "ga2", "ga3", "mix0", "mix1"]
         + ["pt00", "pt01", "pt02", "pt03", "o00", "o01", "gp0", "gp1", "gp2"]
         + ["pt10", "pt11", "pt12", "pt13", "o10", "o11", "gp3"]
         + ["yp0", "yp1", "yp2", "yp3", "ya0", "ya1", "ya2", "ya3"]
         + ["h00", "h01", "h10", "h11", "t0", "t1", "t2", "t3", "logits", "rank"])


def turn(name):
    t = TURNS.index(name)
    return t % 4, t // 4


def build_layer(nc, x, w_in, b_in, sinks, w_o_attn, w_pool_mix, pool_scale, w_o_pool, w_out, ln1_g, ln1_b,
                w_router, b_router, w_gu, b_gu, w_down, b_down, ln2_g, ln2_b, out):
    ctx = ExitStack()
    with ctx:
        def sb(name, shape, dt=F32):
            return ctx.enter_context(nc.sbuf_tensor(name, shape, dt))

        def sem(name):
            return ctx.enter_context(nc.semaphore(name))

        ring = sb("ring", [P, SLOTS, SLOT])
        xs = sb("xs", [P, NT, D])
        feat = sb("feat", [P, KD, CH + SEQ])
        qln = sb("qln", [P, 2 * D])
        kT = sb("kT", [P, SEQ])
        vs = sb("vs", [P, 4, P])
        uT = sb("uT", [P, NG, PAD + SEQ])
        rT = sb("rT", [P, NG, SEQ])
        gates = sb("gates", [P, 2, KD, SEQ])
        probs = sb("probs", [P, NT, NH * P])
        work = sb("work", [P, 2 * NH * P])
        oT = sb("oT", [P, 2 * NG * (PAD + SEQ)])
        ident = sb("ident", [P, P])
        before = sb("before", [P, P])
        ones = sb("ones", [P, P])
        slot_no = sb("slot_no", [P, 2, CAP])
        zeros = sb("zeros", [P, 512], BF16)
        wmix = sb("wmix", [P, NG, P])
        wrt = sb("wrt", [P, KD, NE])
        rows = sb("rows", [33, P])
        cols = sb("cols", [P, 33])
        bv = sb("bv", [P, P])
        sink_b = sb("sink_b", [P, NH])
        br_b = sb("br_b", [P, NE])
        inv_n = sb("inv_n", [P, PAD])
        smax = sb("smax", [P, NT, NH])
        ssum = sb("ssum", [P, NT, NH])
        sden = sb("sden", [P, NT, NH])
        stats = sb("stats", [P, NT, 2, 6])
        mv = sb("mv", [P, NT, 2])
        rstd = sb("rstd", [P, NT, 1])
        logit = sb("logit", [P, NT, NE])
        top = sb("top", [P, NT, 8])
        topi = sb("topi", [P, NT, 8], U32)
        topf = sb("topf", [P, NT, TOPK])
        tex = sb("tex", [P, NT, TOPK])
        tsum = sb("tsum", [P, NT])
        hit = sb("hit", [P, NT, TOPK, NE])
        hitg = sb("hitg", [P, NT, TOPK, NE])
        chosen = sb("chosen", [P, NT, NE])
        gate1 = sb("gate1", [P, NT, NE])
        rank1 = sb("rank1", [P, NT, NE])
        rank_n = sb("rank_n", [P, NT, ROUNDS * NE + 1])
        gate_n = sb("gate_n", [P, NT, ROUNDS * NE])
        most = sb("most", [P, 1])
        most_i = sb("most_i", [P, 1], I32)

        qT = qln[:, :].rearrange("p (m s) -> p m s", m=KD)
        ln_g, ln_b = qln[:, 0:D], qln[:, D:2 * D]
        mT = feat[:, :, 0:SEQ]
        sums = [oT[:, i * NG * (PAD + SEQ):(i + 1) * NG * (PAD + SEQ)].rearrange("p (g s) -> p g s", g=NG)
                for i in range(2)]
        o_heads = oT[:, 0:KD * SEQ].rearrange("p (m s) -> p m s", m=KD)
        kv_w = work[:, 0:SLOT].rearrange("p (k n) -> p k n", k=KD)
        probsT = [work[:, t * NH * P:(t + 1) * NH * P].rearrange("p (h q) -> p h q", h=NH) for t in range(NT)]
        bgu_all = probs[0:NE, 0, :]
        bdn_all = probs[0:NE, 1, 0:D]
        xg = work[:, 0:512].rearrange("p (k j) -> p k j", k=KD)
        gate_c = work[:, 512:1024]
        up_c = work[:, 1024:1536]
        sig = work[:, 1536:2048]
        act_v = work[:, 2048:2560]
        actT = work[:, 2560:3072].rearrange("p (f h j) -> p f h j", f=4, h=2)
        ye = work[:, 3072:3584]
        spreadT = work[:, 3584:3840].rearrange("p (t q) -> p t q", t=NT)
        pick = gates[:, 0, 0, 0:NT * CAP].rearrange("p (t j) -> p t j", t=NT)
        spread = gates[:, 0, 1, 0:NT * P].rearrange("p (t j) -> p t j", t=NT)
        one_e = gates[0:NE, 0, 2, 0:CAP]

        wide = ctx.enter_context(nc.psum_tensor("wide", [P, 4, 512], F32))
        bank = [ctx.enter_context(nc.psum_tensor(f"bank{i}", [P, 512], F32)) for i in range(4)]
        scores = wide[:, :, :].rearrange("p b (h k) -> p (b h) k", k=P)
        gate_ps, up_ps, down_ps, turn_ps = bank

        consts = sem("consts")
        x_in = [sem(f"x_in{t}") for t in range(NT)]
        small_in = sem("small_in")
        late_in = sem("late_in")
        mix_in = {}
        bank_full = [sem(f"bank_full{i}") for i in range(4)]
        bank_free = [sem(f"bank_free{i}") for i in range(4)]
        mask_set = sem("mask_set")
        scores_ready = sem("scores_ready")
        scores_read = sem("scores_read")
        shifted = sem("shifted")
        exps_ready = sem("exps_ready")
        probs_ready = sem("probs_ready")
        probs_used = sem("probs_used")
        kv_used = sem("kv_used")
        pooled = sem("pooled")
        q_used = sem("q_used")
        merged = sem("merged")
        var_ready = sem("var_ready")
        std_ready = sem("std_ready")
        normed = sem("normed")
        ln1_in = sem("ln1_in")
        ln2_in = sem("ln2_in")
        bias_in = sem("bias_in")
        top_shift = sem("top_shift")
        top_exp = sem("top_exp")
        chosen_ready = sem("chosen_ready")
        flag_ready = sem("flag_ready")
        zeros_ready = sem("zeros_ready")
        dve_step = sem("dve_step")
        act_step = sem("act_step")
        slot_free = [sem(f"slot_free{i}") for i in range(SLOTS)]
        slot_full = [sem(f"slot_full{i}") for i in range(SLOTS)]
        pick_ready = sem("pick_ready")
        spread_ready = sem("spread_ready")
        one_ready = sem("one_ready")
        gathered = sem("gathered")
        xg_ready = sem("xg_ready")
        gu_done = sem("gu_done")
        gate_clamped = sem("gate_clamped")
        up_clamped = sem("up_clamped")
        gated = sem("gated")
        sig_ready = sem("sig_ready")
        act_ready = sem("act_ready")
        act_turned = sem("act_turned")
        actT_ready = sem("actT_ready")
        spread_turned = sem("spread_turned")
        spreadT_ready = sem("spreadT_ready")
        down_done = sem("down_done")
        ye_ready = sem("ye_ready")
        combined = sem("combined")
        moe_done = sem("moe_done")
        out_done = sem("out_done")

        w_in_v = w_in[0].rearrange("(k p) n -> p k n", p=P)

        def slot(i, **kw):
            return ring[:, i, :].rearrange("p (k n) -> p k n", **kw)

        MIX = ([f"q{j}" for j in range(4)] + ["u0", "u1"] + [f"ga{j}" for j in range(4)]
               + [f"gp{j}" for j in range(4)] + ["op0", "op1"] + [f"oa{j}" for j in range(4)]
               + [f"wo{j}" for j in range(4)])
        assert len(MIX) == 2 * SLOTS
        for name in MIX + ["kv"]:
            mix_in[name] = sem(f"in_{name}")

        block = ctx.enter_context(nc.Block())

        @block.sync
        def _(sp):
            for t in range(NT):
                sp.dma_start(xs[:, t, :], x[0, t * P:(t + 1) * P, :]).then_inc(x_in[t], 16)
            sp.dma_start(kv_w, w_in_v[:, :, KV0:U0]).then_inc(mix_in["kv"], 16)
            woa = w_o_attn[0].rearrange("(g k p) n -> g p k n", g=NKV, p=HD)
            wop = w_o_pool[0].rearrange("(k p) n -> p k n", p=P)
            wo = w_out[0].rearrange("(k p) n -> p k n", p=P)
            for i, name in enumerate(MIX):
                s, j = i % SLOTS, int(name[-1])
                if i >= SLOTS:
                    sp.wait_ge(slot_free[s], 1)
                got = mix_in[name]
                if name[0] == "q":
                    for g in range(NKV):
                        sp.dma_start(slot(s, k=KD)[:, :, g * P:(g + 1) * P],
                                     w_in_v[:, :, g * 512 + j * P:g * 512 + (j + 1) * P]).then_inc(got, 16)
                elif name[:2] in ("u0", "u1"):
                    sp.dma_start(slot(s, k=KD), w_in_v[:, :, U0 + j * 256:U0 + (j + 1) * 256]).then_inc(got, 16)
                elif name[:2] in ("ga", "gp"):
                    c0 = (GA0 if name[1] == "a" else GP0) + j * 256
                    sp.dma_start(slot(s, k=KD), w_in_v[:, :, c0:c0 + 256]).then_inc(got, 16)
                elif name[:2] == "op":
                    sp.dma_start(slot(s, k=NG), wop[:, :, j * 512:(j + 1) * 512]).then_inc(got, 16)
                elif name[:2] == "oa":
                    for g in range(NKV):
                        sp.dma_start(ring[g * HD:(g + 1) * HD, s, :].rearrange("p (k n) -> p k n", k=KD),
                                     woa[g, :, :, j * 256:(j + 1) * 256]).then_inc(got, 16)
                else:
                    sp.dma_start(slot(s, k=2), wo[:, 2 * j:2 * j + 2, :]).then_inc(got, 16)
            sp.wait_ge(scores_ready, 2)
            sp.dma_start(ln_g, ln1_g[0].partition_broadcast(P)).then_inc(ln1_in, 16)
            sp.dma_start(ln_b, ln1_b[0].partition_broadcast(P)).then_inc(ln1_in, 16)
            sp.wait_ge(probs_used, 2)
            sp.dma_start(bgu_all, b_gu[0]).then_inc(bias_in, 16)
            sp.dma_start(bdn_all, b_down[0]).then_inc(bias_in, 16)

            gu_v = w_gu[0].rearrange("e (k p) n -> e k p n", p=P)
            dn_v = w_down[0].rearrange("e (j k p) n -> e j p k n", k=2, p=P)

            def load_expert(n, e):
                for i in range(SLOTS):
                    sp.wait_ge(slot_free[i], n + 2)
                    if i < GU_CHUNKS:
                        sp.dma_start(ring[:, i, :], gu_v[e, i]).then_inc(slot_full[i], 16)
                    else:
                        sp.dma_start(slot(i, k=2), dn_v[e, i - GU_CHUNKS]).then_inc(slot_full[i], 16)

            with sp.Fori(0, NE) as e:
                load_expert(e, e)
            sp.wait_ge(flag_ready, 1)
            over = sp.value_load(most_i[0:1, 0:1], min_val=0, max_val=SEQ)
            with sp.If(over > CAP):
                with sp.Fori(1, ROUNDS) as r:
                    with sp.Fori(0, NE) as e:
                        load_expert(r * NE + e, e)
            for t in range(NT):
                sp.wait_ge(normed, NT + t + 1)
                sp.dma_start(out[0, t * P:(t + 1) * P, :], xs[:, t, :]).then_inc(out_done, 16)
            sp.wait_ge(out_done, 16 * NT)

        @block.gpsimd
        def _(pool):
            pool.memset(ident[:, :], 0.0).then_inc(consts, 1)
            pool.memset(ones[:, :], 1.0).then_inc(consts, 1)
            pool.wait_ge(consts, 2)
            pool.affine_select(out=ident[:, :], in_=ident[:, :], compare_op=ALU.not_equal, fill=1.0, base=0,
                               pattern=[[-1, P]], channel_multiplier=1).then_inc(consts, 1)
            pool.affine_select(out=before[:, :], in_=ones[:, :], compare_op=ALU.is_gt, fill=0.0, base=0,
                               pattern=[[1, P]], channel_multiplier=-1).then_inc(consts, 1)
            pool.iota(slot_no[:, :, :], pattern=[[0, 2], [1, CAP]], base=0, channel_multiplier=0,
                      allow_small_or_imprecise_dtypes=True).then_inc(consts, 1)
            pool.iota(inv_n[:, :], pattern=[[1, PAD]], base=1, channel_multiplier=0,
                      allow_small_or_imprecise_dtypes=True).then_inc(consts, 1)
            pool.memset(feat[:, :, 0:CH], 0.0).then_inc(consts, 1)
            pool.memset(uT[:, :, 0:PAD], 0.0).then_inc(consts, 1)
            for s in sums:
                pool.memset(s[:, :, 0:PAD], 0.0).then_inc(consts, 1)
            pool.memset(zeros[:, :], 0.0).then_inc(consts, 1)
        CONSTS = 11

        @block.scalar
        def _(act):
            b = b_in[0]
            qb = b[0:D].rearrange("(g m c) -> g m c", g=NKV, c=HD)
            for g in range(NKV):
                act.dma_start(rows[0:8, g * HD:(g + 1) * HD], qb[g]).then_inc(small_in, 16)
            act.dma_start(rows[8:9, :], b[KV0:KV0 + P].rearrange("(m c) -> m c", c=P)).then_inc(small_in, 16)
            act.dma_start(rows[9:29, :], b[U0:].rearrange("(m c) -> m c", c=P)).then_inc(small_in, 16)
            act.dma_start(rows[29:33, :], pool_scale[0].rearrange("(m c) -> m c", c=P)).then_inc(small_in, 16)
            act.dma_start(bv[:, :], b[KV0 + P:U0].partition_broadcast(P)).then_inc(small_in, 16)
            act.dma_start(sink_b[:, :], sinks[0].partition_broadcast(P)).then_inc(small_in, 16)
            act.dma_start(wmix[:, :, :], w_pool_mix[0].rearrange("g c d -> c g d")).then_inc(late_in, 16)
            act.dma_start(wrt[:, :, :], w_router[0].rearrange("(k p) e -> p k e", p=P)).then_inc(late_in, 16)
            act.dma_start(br_b[:, :], b_router[0].partition_broadcast(P)).then_inc(late_in, 16)

            def full(name):
                i, before_ = turn(name)
                act.wait_ge(bank_full[i], before_ + 1)
                return bank[i]

            def free(name):
                return bank_free[turn(name)[0]]

            def turn_x(c):
                t, g = c // 2, c % 2
                ps = full(f"x{c}")
                if c == 0:
                    act.wait_ge(consts, CONSTS)
                act.activation(feat[:, 4 * g:4 * g + 4, CH + t * P:CH + (t + 1) * P],
                               ps[:, :].rearrange("p (k s) -> p k s", k=4), ACT.Copy).then_inc(free(f"x{c}"), 1)

            turn_x(0)
            turn_x(2)
            for j in range(4):
                ps = full(f"q{j}")
                if j == 0:
                    act.wait_ge(bank_free[turn("rows")[0]], turn("rows")[1] + 1)
                for i in range(2):
                    m = 2 * j + i
                    ins = act.activation(qT[:, m, :], ps[:, i * SEQ:(i + 1) * SEQ], ACT.Identity,
                                         bias=cols[:, m:m + 1])
                ins.then_inc(free(f"q{j}"), 1)

            for t in range(NT):
                act.wait_ge(shifted, t + 1)
                act.activation(probs[:, t, :], probs[:, t, :], ACT.Exp).then_inc(act_step, 1)
                act.activation(sden[:, t, :], sden[:, t, :], ACT.Exp).then_inc(exps_ready, 1)

            def sigmoid(a, j):
                name = f"g{'ap'[a]}{j}"
                ps = full(name)
                for i in range(2):
                    m = 2 * j + i
                    c = 13 + a * KD + m
                    ins = act.activation(gates[:, a, m, :], ps[:, i * SEQ:(i + 1) * SEQ], ACT.Sigmoid,
                                         bias=cols[:, c:c + 1])
                ins.then_inc(free(name), 1)

            def turn_probs(t):
                for c in (0, 2):
                    name = f"pt{t}{c}"
                    ps = full(name)
                    if t == 0 and c == 0:
                        act.wait_ge(kv_used, 1)
                    act.activation(probsT[t][:, 4 * c:4 * c + 4, :],
                                   ps[:, :].rearrange("p (h q) -> p h q", h=4), ACT.Copy).then_inc(free(name), 1)

            for j in range(4):
                sigmoid(0, j)
            turn_probs(0)
            for j in range(3):
                sigmoid(1, j)
            turn_probs(1)
            sigmoid(1, 3)

            def root(i):
                act.wait_ge(var_ready, i + 1)
                act.activation(rstd[:, i % NT, :], rstd[:, i % NT, :], ACT.Sqrt).then_inc(std_ready, 1)

            for t in range(NT):
                root(t)
            for c in (0, 2):
                t, g = c // 2, c % 2
                ps = full(f"t{c}")
                act.activation(feat[:, 4 * g:4 * g + 4, t * P:(t + 1) * P],
                               ps[:, :].rearrange("p (k s) -> p k s", k=4), ACT.Copy).then_inc(free(f"t{c}"), 1)
            act.wait_ge(normed, NT)
            act.dma_start(ln_g, ln2_g[0].partition_broadcast(P)).then_inc(ln2_in, 16)
            act.dma_start(ln_b, ln2_b[0].partition_broadcast(P)).then_inc(ln2_in, 16)
            act.wait_ge(top_shift, 1)
            act.activation(tex[:, :, :], tex[:, :, :], ACT.Exp).then_inc(top_exp, 1)

            def take_gathered(n):
                act.wait_ge(gathered, n + 1)
                act.activation(xg, turn_ps[:, :].rearrange("p (k j) -> p k j", k=KD), ACT.Copy).then_inc(xg_ready, 1)

            def expert(n):
                act.wait_ge(gate_clamped, n + 1)
                act.activation(sig, gate_c, ACT.Sigmoid, scale=SW_ALPHA).then_inc(sig_ready, 1)
                take_gathered(n + 1)
                act.wait_ge(spread_turned, n + 1)
                act.activation(spreadT, gate_ps[:, 0:NT * P].rearrange("p (t q) -> p t q", t=NT),
                               ACT.Copy).then_inc(spreadT_ready, 1)
                act.wait_ge(down_done, n + 1)
                act.activation(ye, down_ps[:, :], ACT.Copy).then_inc(ye_ready, 1)

            take_gathered(0)
            with act.Fori(0, NE) as e:
                expert(e)
            act.wait_ge(flag_ready, 1)
            over = act.value_load(most_i[0:1, 0:1], min_val=0, max_val=SEQ)
            with act.If(over > CAP):
                with act.Fori(1, ROUNDS) as r:
                    with act.Fori(0, NE) as e:
                        expert(r * NE + e)
            for t in range(NT):
                root(NT + t)

        @block.tensor
        def _(pe):
            pe.wait_ge(consts, CONSTS)

            def take(name):
                i, before_ = turn(name)
                if before_:
                    pe.wait_ge(bank_free[i], before_)
                return bank[i]

            def full(name):
                return bank_full[turn(name)[0]]

            for c in range(4):
                t, g = c // 2, c % 2
                pe.wait_ge(x_in[t], 16)
                ps = take(f"x{c}")
                for k in range(4):
                    mm = pe.transpose(ps[:, k * P:(k + 1) * P], xs[:, t, (4 * g + k) * P:(4 * g + k + 1) * P],
                                      ident[:, :])
                mm.then_inc(full(f"x{c}"), 1)
            pe.wait_ge(small_in, 7 * 16)
            pe.transpose(take("rows")[:, 0:33], rows[:, :], ident[0:33, 0:33]).then_inc(full("rows"), 1)

            xT = feat[:, :, CH:CH + SEQ]
            ps = take("k")
            for c in range(4):
                pe.wait_ge(bank_free[turn(f"x{c}")[0]], turn(f"x{c}")[1] + 1)
            pe.wait_ge(mix_in["kv"], 16)
            for k in range(KD):
                mm = pe.matmul(ps[:, 0:SEQ], kv_w[:, k, 0:P], xT[:, k, :], start=(k == 0), stop=(k == KD - 1))
            mm.then_inc(full("k"), 1)
            ps = take("v")
            for c in range(4):
                for k in range(KD):
                    mm = pe.matmul(ps[:, c * P:(c + 1) * P], feat[:, k, c * CH:c * CH + P], kv_w[:, k, P:2 * P],
                                   start=(k == 0), stop=(k == KD - 1))
            mm.then_inc(full("v"), 1)

            def project(name, s, weight, rhs, ks, in_count=16, last_use=True):
                ps = take(name)
                for i in range(2):
                    for k in range(ks):
                        mm = pe.matmul(ps[:, i * SEQ:(i + 1) * SEQ], weight(k, i), rhs(k),
                                       start=(k == 0), stop=(k == ks - 1))
                mm.then_inc(full(name), 1)

            def from_x(name):
                s = MIX.index(name) % SLOTS
                if name[0] == "q":
                    pe.wait_ge(mix_in[name], 32)
                    ps = take(name)
                    for i in range(2):
                        for k in range(KD):
                            for g in range(NKV):
                                mm = pe.matmul(ps[g * HD:(g + 1) * HD, i * SEQ:(i + 1) * SEQ],
                                               slot(s, k=KD)[:, k, g * P + i * HD:g * P + (i + 1) * HD],
                                               xT[:, k, :], start=(k == 0), stop=(k == KD - 1))
                    mm.then_inc(full(name), 1)
                else:
                    pe.wait_ge(mix_in[name], 16)
                    project(name, s, lambda k, i: slot(s, k=KD)[:, k, i * P:(i + 1) * P],
                            lambda k: xT[:, k, :], KD)

            def release(name):
                i, before_ = turn(name)
                pe.wait_ge(bank_full[i], before_ + 1)
                pe.sem_inc(slot_free[MIX.index(name) % SLOTS], 1)

            def score(t):
                if t == 0:
                    pe.wait_ge(mask_set, 1)
                    for name in ("k", "q0", "q1", "q2", "q3"):
                        pe.wait_ge(bank_free[turn(name)[0]], turn(name)[1] + 1)
                else:
                    pe.wait_ge(scores_read, 1)
                for m in range(KD):
                    for g in range(NKV):
                        rows_ = slice(g * HD, (g + 1) * HD)
                        for half in range(2):
                            c = 2 * t + half
                            lo = CH if c == 0 else 0
                            mm = pe.matmul(scores[half * CH:(half + 1) * CH, g * KD + m, lo:P],
                                           qT[rows_, m, c * CH:(c + 1) * CH],
                                           kT[rows_, (c - 1) * CH + lo:(c + 1) * CH], start=True, stop=True)
                mm.then_inc(scores_ready, 1)

            def turn_probs(t):
                pe.wait_ge(probs_ready, t + 1)
                for c in range(4):
                    name = f"pt{t}{c}"
                    ps = take(name)
                    for h in range(4):
                        mm = pe.transpose(ps[:, h * P:(h + 1) * P],
                                          probs[:, t, (4 * c + h) * P:(4 * c + h + 1) * P], ident[:, :])
                    mm.then_inc(full(name), 1)

            def attend(t):
                for c in range(4):
                    pe.wait_ge(bank_free[turn(f"pt{t}{c}")[0]], turn(f"pt{t}{c}")[1] + 1)
                for half in range(2):
                    c = 2 * t + half
                    name = f"o{t}{half}"
                    ps = take(name)
                    for g in range(NKV):
                        mm = pe.matmul(ps[g * HD:(g + 1) * HD, :], vs[:, c, g * HD:(g + 1) * HD],
                                       probsT[t][:, g * KD:(g + 1) * KD, half * CH:(half + 1) * CH],
                                       start=True, stop=True)
                    mm.then_inc(full(name), 1)

            for j in range(4):
                from_x(f"q{j}")
                release(f"q{j}")
            score(0)
            for name in ("u0", "u1"):
                from_x(name)
                release(name)
            score(1)
            for j in range(4):
                from_x(f"ga{j}")
                release(f"ga{j}")
            pe.wait_ge(late_in, 3 * 16)
            pe.wait_ge(pooled, NG)
            for j in range(2):
                ps = take(f"mix{j}")
                for i in range(2):
                    g = 2 * j + i
                    mm = pe.matmul(ps[:, i * SEQ:(i + 1) * SEQ], wmix[:, g, :], rT[:, g, :], start=True, stop=True)
                mm.then_inc(full(f"mix{j}"), 1)
            turn_probs(0)
            attend(0)
            for j in range(3):
                from_x(f"gp{j}")
                release(f"gp{j}")
            turn_probs(1)
            attend(1)
            from_x("gp3")
            release("gp3")
            for j in range(2):
                pe.wait_ge(bank_free[turn(f"mix{j}")[0]], turn(f"mix{j}")[1] + 1)
            for j in range(4):
                s = MIX.index(f"op{j // 2}") % SLOTS
                pe.wait_ge(mix_in[f"op{j // 2}"], 16)
                project(f"yp{j}", s,
                        lambda k, i: slot(s, k=NG)[:, k, (j % 2) * 256 + i * P:(j % 2) * 256 + (i + 1) * P],
                        lambda k: uT[:, k, PAD:PAD + SEQ], NG)
                if j % 2:
                    pe.wait_ge(full(f"yp{j}"), turn(f"yp{j}")[1] + 1)
                    pe.sem_inc(slot_free[s], 1)
            for t in range(NT):
                for half in range(2):
                    pe.wait_ge(bank_free[turn(f"o{t}{half}")[0]], turn(f"o{t}{half}")[1] + 1)
            for j in range(4):
                s = MIX.index(f"oa{j}") % SLOTS
                pe.wait_ge(mix_in[f"oa{j}"], 32)
                project(f"ya{j}", s, lambda k, i: slot(s, k=KD)[:, k, i * P:(i + 1) * P],
                        lambda k: o_heads[:, k, :], KD)
                pe.wait_ge(full(f"ya{j}"), turn(f"ya{j}")[1] + 1)
                pe.sem_inc(slot_free[s], 1)
            pe.wait_ge(merged, 4)
            for j in range(4):
                pe.wait_ge(mix_in[f"wo{j}"], 16)
            for t in range(NT):
                for half in range(2):
                    name = f"h{t}{half}"
                    ps = take(name)
                    for k in range(KD):
                        s = MIX.index(f"wo{k // 2}") % SLOTS
                        mm = pe.matmul(ps[:, :], mT[:, k, t * P:(t + 1) * P],
                                       slot(s, k=2)[:, k % 2, half * 512:(half + 1) * 512],
                                       start=(k == 0), stop=(k == KD - 1))
                    mm.then_inc(full(name), 1)
            pe.wait_ge(full("h11"), turn("h11")[1] + 1)
            for j in range(4):
                pe.sem_inc(slot_free[MIX.index(f"wo{j}") % SLOTS], 1)
            for c in range(4):
                t, g = c // 2, c % 2
                pe.wait_ge(normed, t + 1)
                ps = take(f"t{c}")
                for k in range(4):
                    mm = pe.transpose(ps[:, k * P:(k + 1) * P], xs[:, t, (4 * g + k) * P:(4 * g + k + 1) * P],
                                      ident[:, :])
                mm.then_inc(full(f"t{c}"), 1)
            ps = take("logits")
            for c in range(4):
                pe.wait_ge(bank_free[turn(f"t{c}")[0]], turn(f"t{c}")[1] + 1)
            for t in range(NT):
                for k in range(KD):
                    mm = pe.matmul(ps[:, t * NE:(t + 1) * NE], mT[:, k, t * P:(t + 1) * P], wrt[:, k, :],
                                   start=(k == 0), stop=(k == KD - 1))
            mm.then_inc(full("logits"), 1)
            for i in range(4):
                pe.matmul(wide[:, i, :], zeros[:, 0:P], zeros[:, :], start=True, stop=False, skip_group_check=True)
            ps = take("rank")
            pe.wait_ge(chosen_ready, 1)
            pe.matmul(ps[:, 0:NE], before[:, :], chosen[:, 0, :], start=True, stop=True)
            pe.matmul(ps[:, NE:2 * NE], ones[:, :], chosen[:, 0, :], start=True, stop=False)
            pe.matmul(ps[:, NE:2 * NE], before[:, :], chosen[:, 1, :], start=False, stop=True)
            pe.matmul(ps[:, 2 * NE:3 * NE], ones[:, :], chosen[:, 0, :], start=True, stop=False)
            pe.matmul(ps[:, 2 * NE:3 * NE], ones[:, :], chosen[:, 1, :], start=False,
                      stop=True).then_inc(full("rank"), 1)
            pe.wait_ge(bias_in, 32)

            def gather(n):
                pe.wait_ge(pick_ready, n + 1)
                for k in range(KD):
                    for t in range(NT):
                        mm = pe.matmul(turn_ps[:, k * CAP:(k + 1) * CAP], xs[:, t, k * P:(k + 1) * P],
                                       pick[:, t, :], start=(t == 0), stop=(t == NT - 1))
                mm.then_inc(gathered, 1)

            def combine(stop):
                for t in range(NT):
                    for half in range(2):
                        part = slice(half * CAP, (half + 1) * CAP)
                        mm = pe.matmul(wide[:, 2 * t + half, :], spreadT[part, t, :], ye[part, :],
                                       start=False, stop=stop, skip_group_check=True)
                return mm

            def expert(n):
                pe.wait_ge(xg_ready, n + 1)
                pe.wait_ge(spreadT_ready, n + 1)
                for k in range(GU_CHUNKS):
                    pe.wait_ge(slot_full[k], 16 * n + 16)
                    for c, ps in enumerate((gate_ps, up_ps)):
                        for half in range(2):
                            col = (2 * c + half) * 512
                            mm = pe.matmul(ps[half * CAP:(half + 1) * CAP, :], xg[:, k, :],
                                           ring[:, k, col:col + 512], start=(k == 0), stop=False)
                    mm.then_inc(slot_free[k], 1)
                pe.wait_ge(one_ready, n + 1)
                for c, ps in enumerate((gate_ps, up_ps)):
                    for half in range(2):
                        col = (2 * c + half) * 512
                        mm = pe.matmul(ps[half * CAP:(half + 1) * CAP, :], one_e, bgu_all[:, col:col + 512],
                                       start=False, stop=True)
                mm.then_inc(gu_done, 1)
                pe.wait_ge(actT_ready, n + 1)
                gather(n + 1)
                pe.wait_ge(ye_ready, n + 1)
                combine(False).then_inc(combined, 1)
                pe.wait_ge(act_ready, n + 1)
                pe.wait_ge(xg_ready, n + 2)
                for f in range(4):
                    mm = pe.transpose(turn_ps[:, f * P:(f + 1) * P], act_v[:, f * P:(f + 1) * P], ident[:, :])
                mm.then_inc(act_turned, 1)
                pe.wait_ge(spread_ready, n + 1)
                for t in range(NT):
                    mm = pe.transpose(gate_ps[:, t * P:(t + 1) * P], spread[:, t, :], ident[:, :])
                mm.then_inc(spread_turned, 1)
                pe.wait_ge(actT_ready, n + 2)
                for k in range(KD):
                    i = GU_CHUNKS + k // 2
                    if k % 2 == 0:
                        pe.wait_ge(slot_full[i], 16 * n + 16)
                    for half in range(2):
                        mm = pe.matmul(down_ps[half * CAP:(half + 1) * CAP, :], actT[:, k % 4, k // 4, :],
                                       slot(i, k=2)[:, k % 2, half * 512:(half + 1) * 512],
                                       start=(k == 0), stop=False)
                    if k % 2:
                        mm.then_inc(slot_free[i], 1)
                for half in range(2):
                    mm = pe.matmul(down_ps[half * CAP:(half + 1) * CAP, :], one_e,
                                   bdn_all[:, half * 512:(half + 1) * 512], start=False, stop=True)
                mm.then_inc(down_done, 1)

            gather(0)
            with pe.Fori(0, NE) as e:
                expert(e)
            pe.wait_ge(flag_ready, 1)
            over = pe.value_load(most_i[0:1, 0:1], min_val=0, max_val=SEQ)
            with pe.If(over > CAP):
                with pe.Fori(1, ROUNDS) as r:
                    with pe.Fori(0, NE) as e:
                        expert(r * NE + e)
                pe.wait_ge(ye_ready, ROUNDS * NE + 1)
            pe.wait_ge(ye_ready, NE + 1)
            combine(True).then_inc(moe_done, 1)

        @block.vector
        def _(dve):
            done = [0]

            def then(ins):
                done[0] += 1
                ins.then_inc(dve_step, 1)
                dve.wait_ge(dve_step, done[0])

            def full(name):
                i, before_ = turn(name)
                dve.wait_ge(bank_full[i], before_ + 1)
                return bank[i]

            def free(name):
                return bank_free[turn(name)[0]]

            dve.memset(scores[0:CH, :, 0:CH], NEG).then_inc(mask_set, 1)
            dve.wait_ge(consts, CONSTS)
            then(dve.reciprocal(inv_n[:, :], inv_n[:, :]))
            for c in (1, 3):
                t, g = c // 2, c % 2
                ps = full(f"x{c}")
                dve.tensor_copy(feat[:, 4 * g:4 * g + 4, CH + t * P:CH + (t + 1) * P],
                                ps[:, :].rearrange("p (k s) -> p k s", k=4)).then_inc(free(f"x{c}"), 1)
            ps = full("rows")
            dve.tensor_copy(cols[:, :], ps[:, 0:33]).then_inc(free("rows"), 1)
            dve.wait_ge(free("rows"), turn("rows")[1] + 1)
            ps = full("k")
            dve.tensor_scalar(kT[:, :], ps[:, 0:SEQ], cols[:, 8:9], None, ALU.add).then_inc(free("k"), 1)
            ps = full("v")
            dve.tensor_tensor(vs[:, :, :], ps[:, :].rearrange("p (c n) -> p c n", c=4),
                              bv[:, :].unsqueeze(1).to_broadcast([P, 4, P]), ALU.add).then_inc(free("v"), 1)
            dve.wait_ge(free("v"), turn("v")[1] + 1)
            dve.sem_inc(kv_used, 1)

            def softmax_shift(t):
                dve.wait_ge(scores_ready, t + 1)
                then(dve.tensor_reduce(smax[:, t, :], scores, AX.X, ALU.max))
                then(dve.scalar_tensor_tensor(out=smax[:, t, :], in0=smax[:, t, :], scalar=HD ** -0.5,
                                              in1=sink_b[:, :], op0=ALU.mult, op1=ALU.max))
                dve.tensor_tensor(sden[:, t, :], sink_b[:, :], smax[:, t, :], ALU.subtract).then_inc(dve_step, 1)
                done[0] += 1
                then(dve.scalar_tensor_tensor(out=probs[:, t, :].rearrange("p (h k) -> p h k", h=NH), in0=scores,
                                              scalar=HD ** -0.5,
                                              in1=smax[:, t, :].unsqueeze(2).to_broadcast([P, NH, P]),
                                              op0=ALU.mult, op1=ALU.subtract))
                dve.sem_inc(scores_read, 1)
                dve.sem_inc(shifted, 1)

            def softmax_norm(t):
                p3 = probs[:, t, :].rearrange("p (h k) -> p h k", h=NH)
                dve.wait_ge(act_step, t + 1)
                dve.wait_ge(exps_ready, t + 1)
                then(dve.tensor_reduce(ssum[:, t, :], p3, AX.X, ALU.add))
                then(dve.tensor_tensor(sden[:, t, :], sden[:, t, :], ssum[:, t, :], ALU.add))
                then(dve.reciprocal(sden[:, t, :], sden[:, t, :]))
                dve.tensor_tensor(p3, p3, sden[:, t, :].unsqueeze(2).to_broadcast([P, NH, P]),
                                  ALU.mult).then_inc(probs_ready, 1)

            softmax_shift(0)
            for j in range(2):
                ps = full(f"u{j}")
                for i in range(2):
                    g = 2 * j + i
                    ins = dve.tensor_scalar(uT[:, g, PAD:], ps[:, i * SEQ:(i + 1) * SEQ], cols[:, 9 + g:10 + g],
                                            None, ALU.add)
                ins.then_inc(free(f"u{j}"), 1)
            dve.wait_ge(free("u1"), turn("u1")[1] + 1)
            softmax_shift(1)
            softmax_norm(0)
            src = uT
            for step in range(NG):
                w = 1 << step
                dst = sums[step % 2]
                then(dve.tensor_tensor(dst[:, step:, PAD:], src[:, step:, PAD:], src[:, step:, PAD - w:PAD + SEQ - w],
                                       ALU.add))
                src = dst
            for g in range(NG):
                w = 2 << g
                s = sums[g % 2]
                then(dve.scalar_tensor_tensor(out=rT[:, g, :], in0=s[:, g, PAD:], scalar=1.0 / w,
                                              in1=uT[:, g, PAD:], op0=ALU.mult, op1=ALU.subtract))
                then(dve.tensor_tensor(s[:, g, PAD:PAD + w - 1], s[:, g, PAD:PAD + w - 1], inv_n[:, 0:w - 1],
                                       ALU.mult))
                dve.tensor_tensor(rT[:, g, 0:w - 1], s[:, g, PAD:PAD + w - 1], uT[:, g, PAD:PAD + w - 1],
                                  ALU.subtract).then_inc(pooled, 1)
            dve.wait_ge(pooled, NG)
            softmax_norm(1)
            for j in range(2):
                ps = full(f"mix{j}")
                for i in range(2):
                    g = 2 * j + i
                    ins = dve.tensor_scalar(uT[:, g, PAD:], ps[:, i * SEQ:(i + 1) * SEQ], cols[:, 29 + g:30 + g],
                                            None, ALU.mult)
                ins.then_inc(free(f"mix{j}"), 1)

            def turn_probs(t):
                for c in (1, 3):
                    name = f"pt{t}{c}"
                    ps = full(name)
                    dve.tensor_copy(probsT[t][:, 4 * c:4 * c + 4, :],
                                    ps[:, :].rearrange("p (h q) -> p h q", h=4)).then_inc(free(name), 1)
                    if c == 3:
                        dve.sem_inc(probs_used, 1)

            def take_attended(t):
                for half in range(2):
                    c = 2 * t + half
                    name = f"o{t}{half}"
                    ps = full(name)
                    dve.tensor_copy(o_heads[:, :, c * CH:(c + 1) * CH],
                                    ps[:, :].rearrange("p (m q) -> p m q", m=KD)).then_inc(free(name), 1)

            for t in range(NT):
                turn_probs(t)
                take_attended(t)

            for a, branch in ((1, "yp"), (0, "ya")):
                for j in range(4):
                    name = f"{branch}{j}"
                    ps = full(name)
                    gname = f"g{'ap'[a]}{j}"
                    dve.wait_ge(free(gname), turn(gname)[1] + 1)
                    g = gates[:, a, 2 * j:2 * j + 2, :]
                    dve.tensor_tensor(g, g, ps[:, :].rearrange("p (i s) -> p i s", i=2),
                                      ALU.mult).then_inc(free(name), 1)
                    if a == 0:
                        dve.wait_ge(free(name), turn(name)[1] + 1)
                        dve.tensor_tensor(mT[:, 2 * j:2 * j + 2, :], g, gates[:, 1, 2 * j:2 * j + 2, :],
                                          ALU.add).then_inc(merged, 1)

            def layer_norm(t, i, parts, vectors_in):
                for half in range(2):
                    z = xs[:, t, half * 512:(half + 1) * 512]
                    ps, freed = parts(half)
                    ins = dve.scalar_tensor_tensor(out=z, in0=z, scalar=ALPHA, in1=ps, op0=ALU.mult, op1=ALU.add)
                    then(ins)
                    if freed is not None:
                        dve.sem_inc(freed, 1)
                    then(dve.bn_stats(stats[:, t, half, :], z))
                then(dve.bn_aggr(mv[:, t, :], stats[:, t, :, :]))
                dve.tensor_scalar(rstd[:, t, :], mv[:, t, 1:2], EPS, None, ALU.add).then_inc(var_ready, 1)
                dve.wait_ge(std_ready, i + 1)
                then(dve.reciprocal(rstd[:, t, :], rstd[:, t, :]))
                z = xs[:, t, :]
                then(dve.tensor_scalar(z, z, mv[:, t, 0:1], rstd[:, t, :], ALU.subtract, ALU.mult))
                dve.wait_ge(vectors_in, 32)
                then(dve.tensor_tensor(z, z, ln_g, ALU.mult))
                dve.tensor_tensor(z, z, ln_b, ALU.add).then_inc(normed, 1)

            for t in range(NT):
                layer_norm(t, t, lambda half: (full(f"h{t}{half}")[:, :], free(f"h{t}{half}")), ln1_in)
            for c in (1, 3):
                t, g = c // 2, c % 2
                ps = full(f"t{c}")
                dve.tensor_copy(feat[:, 4 * g:4 * g + 4, t * P:(t + 1) * P],
                                ps[:, :].rearrange("p (k s) -> p k s", k=4)).then_inc(free(f"t{c}"), 1)

            ps = full("logits")
            dve.wait_ge(late_in, 3 * 16)
            dve.tensor_tensor(logit[:, :, :], ps[:, 0:NT * NE].rearrange("p (t e) -> p t e", t=NT),
                              br_b[:, :].unsqueeze(1).to_broadcast([P, NT, NE]), ALU.add).then_inc(free("logits"), 1)
            dve.wait_ge(free("logits"), turn("logits")[1] + 1)
            for t in range(NT):
                then(dve.max(top[:, t, :], logit[:, t, :]))
                then(dve.max_index(topi[:, t, :], top[:, t, :], logit[:, t, :]))
            then(dve.tensor_copy(topf[:, :, :], topi[:, :, 0:TOPK]))
            dve.tensor_tensor(tex[:, :, :], top[:, :, 0:TOPK], top[:, :, 0:1].to_broadcast([P, NT, TOPK]),
                              ALU.subtract).then_inc(top_shift, 1)
            expert_no = slot_no[:, 0, 0:NE]
            then(dve.tensor_tensor(hit[:, :, :, :].rearrange("p t s e -> p (t s) e"),
                                   expert_no.unsqueeze(1).to_broadcast([P, NT * TOPK, NE]),
                                   topf[:, :, :].rearrange("p t s -> p (t s)").unsqueeze(2)
                                   .to_broadcast([P, NT * TOPK, NE]), ALU.is_equal))
            dve.tensor_reduce(chosen[:, :, :], hit[:, :, :, :].rearrange("p t s e -> p t e s"), AX.X,
                              ALU.add).then_inc(chosen_ready, 1)
            dve.wait_ge(top_exp, 1)
            then(dve.tensor_reduce(tsum[:, :], tex[:, :, :], AX.X, ALU.add))
            then(dve.reciprocal(tsum[:, :], tsum[:, :]))
            then(dve.tensor_tensor(tex[:, :, :], tex[:, :, :], tsum[:, :].unsqueeze(2).to_broadcast([P, NT, TOPK]),
                                   ALU.mult))
            then(dve.tensor_tensor(hitg[:, :, :, :].rearrange("p t s e -> p (t s) e"),
                                   hit[:, :, :, :].rearrange("p t s e -> p (t s) e"),
                                   tex[:, :, :].rearrange("p t s -> p (t s)").unsqueeze(2)
                                   .to_broadcast([P, NT * TOPK, NE]), ALU.mult))
            then(dve.tensor_reduce(gate1[:, :, :], hitg[:, :, :, :].rearrange("p t s e -> p t e s"), AX.X, ALU.add))
            for r in range(ROUNDS):
                then(dve.tensor_copy(gate_n[:, :, r * NE:(r + 1) * NE], gate1[:, :, :]))
            dve.wait_ge(chosen_ready, 1)
            ps = full("rank")
            then(dve.scalar_tensor_tensor(out=rank1[:, :, :],
                                          in0=ps[:, 0:NT * NE].rearrange("p (t e) -> p t e", t=NT), scalar=1.0,
                                          in1=chosen[:, :, :], op0=ALU.add, op1=ALU.mult))
            then(dve.tensor_reduce(most[:, :], ps[:, NT * NE:(NT + 1) * NE], AX.X, ALU.max))
            dve.tensor_copy(most_i[:, :], most[:, :]).then_inc(flag_ready, 1)
            then(dve.memset(rank_n[:, :, ROUNDS * NE:], -1.0))
            for r in range(ROUNDS):
                then(dve.tensor_scalar(rank_n[:, :, r * NE:(r + 1) * NE], rank1[:, :, :], 1.0 + r * CAP, None,
                                       ALU.subtract))
            dve.memset(ye, 0.0).then_inc(zeros_ready, 1)
            dve.memset(spreadT, 0.0).then_inc(zeros_ready, 1)
            dve.wait_ge(zeros_ready, 2)
            dve.sem_inc(ye_ready, 1)
            dve.sem_inc(spreadT_ready, 1)
            dve.sem_inc(actT_ready, 1)

            def pick_step(n):
                for t in range(NT):
                    ins = dve.tensor_scalar(pick[:, t, :], slot_no[:, 0, :], rank_n[:, t, bass.ds(n, 1)], None,
                                            ALU.is_equal)
                ins.then_inc(pick_ready, 1)

            def expert(n, e):
                dve.wait_ge(down_done, n)
                dve.tensor_copy(one_e, ident[0:NE, bass.ds(e, 1)].to_broadcast([NE, CAP])).then_inc(one_ready, 1)
                dve.wait_ge(gathered, n + 1)
                pick_step(n + 1)
                dve.wait_ge(spread_turned, n)
                for t in range(NT):
                    ins = dve.tensor_scalar(spread[:, t, :], slot_no[:, :, :].rearrange("p a j -> p (a j)"),
                                            rank_n[:, t, bass.ds(n, 1)], gate_n[:, t, bass.ds(n, 1)],
                                            ALU.is_equal, ALU.mult)
                ins.then_inc(spread_ready, 1)
                dve.wait_ge(gu_done, n + 1)
                dve.tensor_scalar(gate_c, gate_ps[:, :], SW_LIMIT, None, ALU.min).then_inc(gate_clamped, 1)
                dve.tensor_scalar(up_c, up_ps[:, :], -SW_LIMIT, SW_LIMIT, ALU.max, ALU.min).then_inc(up_clamped, 1)
                dve.wait_ge(gate_clamped, n + 1)
                dve.wait_ge(up_clamped, n + 1)
                dve.scalar_tensor_tensor(out=up_c, in0=up_c, scalar=1.0, in1=gate_c, op0=ALU.add,
                                         op1=ALU.mult).then_inc(gated, 1)
                dve.wait_ge(gated, n + 1)
                dve.wait_ge(sig_ready, n + 1)
                dve.tensor_tensor(act_v, up_c, sig, ALU.mult).then_inc(act_ready, 1)
                dve.wait_ge(act_turned, n + 1)
                dve.tensor_copy(actT, turn_ps[:, :].rearrange("p (f h j) -> p f h j", f=4, h=2)).then_inc(actT_ready, 1)

            pick_step(0)
            with dve.Fori(0, NE) as e:
                expert(e, e)
            dve.wait_ge(flag_ready, 1)
            over = dve.value_load(most_i[0:1, 0:1], min_val=0, max_val=SEQ)
            with dve.If(over > CAP):
                with dve.Fori(1, ROUNDS) as r:
                    with dve.Fori(0, NE) as e:
                        expert(r * NE + e, e)
            dve.wait_ge(moe_done, 1)
            for t in range(NT):
                layer_norm(t, NT + t, lambda half: (wide[:, 2 * t + half, :], None), ln2_in)


INS = ["x", "w_in", "b_in", "sinks", "w_o_attn", "w_pool_mix", "pool_scale", "w_o_pool", "w_out", "ln1_g", "ln1_b",
       "w_router", "b_router", "w_gu", "b_gu", "w_down", "b_down", "ln2_g", "ln2_b"]


def kernel(**inputs):
    import numpy as np
    import concourse.bacc as bacc
    from concourse.bass_utils import run_bass_kernel_spmd

    nc = bacc.Bacc("TRN2", target_bir_lowering=False, num_devices=1)
    arrays, args = {}, []
    for name in INS:
        a = np.ascontiguousarray(inputs[name])
        arrays[f"in_{name}_dram"] = a
        args.append(nc.dram_tensor(f"in_{name}_dram", a.shape, mybir.dt.from_np(a.dtype), kind="ExternalInput").ap())
    args.append(nc.dram_tensor("out_dram", (1, SEQ, D), F32, kind="ExternalOutput").ap())
    build_layer(nc, *args)
    r = run_bass_kernel_spmd(nc, [arrays], core_ids=[0])
    return r.results[0]["out_dram"]
```

```python
from contextlib import ExitStack

import concourse.bass as bass
from concourse import mybir

F32 = mybir.dt.float32
BF16 = mybir.dt.bfloat16
I32 = mybir.dt.int32
U32 = mybir.dt.uint32
ALU = mybir.AluOpType
ACT = mybir.ActivationFunctionType
AX = mybir.AxisListType

P = 128
D = 1024
SEQ = 256
NT = SEQ // P
KD = D // P
CH = 64
HD = 64
NH = D // HD
NKV = 2
NG = 4
PAD = 16
NE = 32
TOPK = 4
F = D
CAP = 64
ROUNDS = SEQ // CAP
SLOTS = 12
GU_CHUNKS = KD
DN_CHUNKS = KD // 2
SLOT = 2 * D
ALPHA = 2 ** 0.25
EPS = 1e-5
NEG = -1e30
SW_ALPHA = 1.702
SW_LIMIT = 7.0
KV0 = D
U0 = KV0 + 2 * NKV * HD
GA0 = U0 + NG * P
GP0 = GA0 + D

TURNS = (["x0", "x1", "x2", "x3", "k", "v", "rows", "q0", "q1", "q2", "q3", "u0", "u1", "ga0"]
         + ["ga1", "ga2", "ga3", "mix0", "mix1"]
         + ["pt00", "pt01", "pt02", "pt03", "o00", "o01", "gp0", "gp1", "gp2"]
         + ["pt10", "pt11", "pt12", "pt13", "o10", "o11", "gp3"]
         + ["yp0", "yp1", "yp2", "yp3", "ya0", "ya1", "ya2", "ya3"]
         + ["h00", "h01", "h10", "h11", "t0", "t1", "logits0", "t2", "t3", "logits1", "rank"])


def turn(name):
    t = TURNS.index(name)
    return t % 4, t // 4


def build_layer(nc, x, w_in, b_in, sinks, w_o_attn, w_pool_mix, pool_scale, w_o_pool, w_out, ln1_g, ln1_b,
                w_router, b_router, w_gu, b_gu, w_down, b_down, ln2_g, ln2_b, out):
    ctx = ExitStack()
    with ctx:
        def sb(name, shape, dt=F32):
            return ctx.enter_context(nc.sbuf_tensor(name, shape, dt))

        def sem(name):
            return ctx.enter_context(nc.semaphore(name))

        ring = sb("ring", [P, SLOTS, SLOT])
        xs = sb("xs", [P, NT, D])
        feat = sb("feat", [P, KD, SEQ])
        qln = sb("qln", [P, 2 * D])
        kT = sb("kT", [P, SEQ])
        vs = sb("vs", [P, 4, P])
        ur = sb("ur", [P, NG * (PAD + 2 * SEQ)])
        gates = sb("gates", [P, 2, KD, SEQ])
        probs = sb("probs", [P, NT, NH * P])
        work = sb("work", [P, 2 * NH * P])
        bias3 = sb("bias3", [3 * NE, 3 * D], BF16)
        sel3 = sb("sel3", [3 * NE, NE], BF16)
        one_e = sb("one_e", [3 * NE, 2, CAP], BF16)
        oT = sb("oT", [P, 2 * NG * (PAD + SEQ)])
        ident = sb("ident", [P, P])
        before = sb("before", [P, P], BF16)
        ones = sb("ones", [P, P], BF16)
        slot_no = sb("slot_no", [P, 2, CAP])
        zeros = sb("zeros", [P, 512], BF16)
        wmix = sb("wmix", [P, NG, P])
        wrt = sb("wrt", [P, KD, NE])
        rows = sb("rows", [33, P])
        cols = sb("cols", [P, 33])
        bv = sb("bv", [P, P])
        sink_b = sb("sink_b", [P, NH])
        br_b = sb("br_b", [P, NE])
        inv_n = sb("inv_n", [P, PAD])
        smax = sb("smax", [P, NT, NH])
        ssum = sb("ssum", [P, NT, NH])
        sden = sb("sden", [P, NT, NH])
        stats = sb("stats", [P, NT, 2, 6])
        mv = sb("mv", [P, NT, 2])
        rstd = sb("rstd", [P, NT, 1])
        logit = sb("logit", [P, NT, NE])
        top = sb("top", [P, NT, 8])
        topi = sb("topi", [P, NT, 8], U32)
        topf = sb("topf", [P, NT, TOPK])
        tex = sb("tex", [P, NT, TOPK])
        tsum = sb("tsum", [P, NT])
        chosen = sb("chosen", [P, NT, NE], BF16)
        gate1 = sb("gate1", [P, NT, NE])
        rank1 = sb("rank1", [P, NT, NE])
        rank_n = sb("rank_n", [P, NT, ROUNDS * NE + 2])
        gate_n = sb("gate_n", [P, NT, ROUNDS * NE])
        most = sb("most", [P, 1])
        most_i = sb("most_i", [P, 1], I32)

        qT = qln[:, :].rearrange("p (m s) -> p m s", m=KD)
        ln_g, ln_b = qln[:, 0:D], qln[:, D:2 * D]
        uT = ur[:, 0:NG * (PAD + SEQ)].rearrange("p (g s) -> p g s", g=NG)
        rT = ur[:, NG * (PAD + SEQ):].rearrange("p (g s) -> p g s", g=NG)
        hit, hitg = [vs[:, :, :].rearrange("p c n -> p (c n)")[:, i * 256:(i + 1) * 256]
                     .rearrange("p (t s e) -> p t s e", t=NT, s=TOPK) for i in range(2)]
        sums = [oT[:, i * NG * (PAD + SEQ):(i + 1) * NG * (PAD + SEQ)].rearrange("p (g s) -> p g s", g=NG)
                for i in range(2)]
        o_heads = oT[:, 0:KD * SEQ].rearrange("p (m s) -> p m s", m=KD)
        kv_w = work[:, 0:SLOT].rearrange("p (k n) -> p k n", k=KD)
        probsT = [work[:, t * NH * P:(t + 1) * NH * P].rearrange("p (h q) -> p h q", h=NH) for t in range(NT)]
        bias_raw = work[0:3 * NE, 0:3 * D]
        xg = work[:, 0:1024].rearrange("p (k i j) -> p k i j", k=KD, i=2)
        gate_c = work[:, 1024:1536]
        up_c = work[:, 1536:2048]
        sig = work[:, 2048:2560]
        act_v = work[:, 2560:3072]
        actT = work[:, 3072:3584].rearrange("p (f h j) -> p f h j", f=4, h=2)
        spreadT = work[:, 3584:4096].rearrange("p (t h q) -> p t h q", t=NT, h=2)
        flat = feat[:, :, :].rearrange("p k s -> p (k s)")
        ye = [flat[:, h * 512:(h + 1) * 512] for h in range(2)]
        pick = flat[:, 1024:1280].rearrange("p (t i j) -> p t i j", t=NT, i=2)
        spread = flat[:, 1280:1664].rearrange("p (t i j) -> p t i j", t=NT, i=3)
        annex = ([probs[:, t, :] for t in range(NT)] + [ur[:, 0:SLOT], oT[:, 0:SLOT]]
                 + [gates[:, a, :, :].rearrange("p k s -> p (k s)") for a in range(2)])

        wide = ctx.enter_context(nc.psum_tensor("wide", [P, 4, 512], F32))
        bank = [ctx.enter_context(nc.psum_tensor(f"bank{i}", [P, 512], F32)) for i in range(4)]
        scores = wide[:, :, :].rearrange("p b (h k) -> p (b h) k", k=P)
        gate_ps, up_ps, down_ps, turn_ps = bank

        consts = sem("consts")
        x_in = [sem(f"x_in{c}") for c in range(4)]
        small_in = sem("small_in")
        late_in = sem("late_in")
        mix_in = {}
        bank_full = [sem(f"bank_full{i}") for i in range(4)]
        bank_free = [sem(f"bank_free{i}") for i in range(4)]
        mask_set = sem("mask_set")
        scores_ready = sem("scores_ready")
        scores_read = sem("scores_read")
        shifted = sem("shifted")
        exps_ready = sem("exps_ready")
        probs_ready = sem("probs_ready")
        probs_used = sem("probs_used")
        pooled = sem("pooled")
        q_used = sem("q_used")
        merged = sem("merged")
        var_ready = sem("var_ready")
        std_ready = sem("std_ready")
        normed = sem("normed")
        ln1_in = sem("ln1_in")
        ln2_in = sem("ln2_in")
        v_moved = sem("v_moved")
        bias_in = sem("bias_in")
        pool_step = sem("pool_step")
        bias_split = sem("bias_split")
        annex_in = [sem(f"annex_in{i}") for i in range(len(annex))]
        top_shift = sem("top_shift")
        top_exp = sem("top_exp")
        chosen_ready = sem("chosen_ready")
        flag_ready = sem("flag_ready")
        zeros_ready = sem("zeros_ready")
        dve_step = sem("dve_step")
        act_step = sem("act_step")
        slot_free = [sem(f"slot_free{i}") for i in range(SLOTS)]
        slot_full = [sem(f"slot_full{i}") for i in range(SLOTS)]
        pick_ready = sem("pick_ready")
        spread_ready = sem("spread_ready")
        one_ready = sem("one_ready")
        gathered = sem("gathered")
        xg_ready = sem("xg_ready")
        combined = sem("combined")
        gu_done = sem("gu_done")
        gate_clamped = sem("gate_clamped")
        up_clamped = sem("up_clamped")
        gated = sem("gated")
        sig_ready = sem("sig_ready")
        act_ready = sem("act_ready")
        act_turned = sem("act_turned")
        actT_ready = sem("actT_ready")
        spread_turned = sem("spread_turned")
        spreadT_ready = sem("spreadT_ready")
        down_done = sem("down_done")
        ye_ready = sem("ye_ready")
        moe_done = sem("moe_done")
        out_done = sem("out_done")

        w_in_v = w_in[0].rearrange("(k p) n -> p k n", p=P)

        def slot(i, **kw):
            return ring[:, i, :].rearrange("p (k n) -> p k n", **kw)

        MIX = ([f"q{j}" for j in range(4)] + ["u0", "u1"] + [f"ga{j}" for j in range(4)]
               + [f"gp{j}" for j in range(4)] + ["op0", "op1"] + [f"oa{j}" for j in range(4)]
               + [f"wo{j}" for j in range(4)])
        assert len(MIX) == 2 * SLOTS
        LAST = {name: {"op": f"yp{2 * int(name[-1]) + 1}", "oa": f"ya{name[-1]}", "wo": "h11"}.get(name[:2], name)
                for name in MIX}
        for name in MIX + ["kv0", "kv1"]:
            mix_in[name] = sem(f"in_{name}")

        block = ctx.enter_context(nc.Block())

        @block.sync
        def _(sp):
            for c in range(4):
                t, g = c // 2, c % 2
                sp.dma_start(xs[:, t, g * 512:(g + 1) * 512],
                             x[0, t * P:(t + 1) * P, g * 512:(g + 1) * 512]).then_inc(x_in[c], 16)
            for g in range(2):
                sp.dma_start(kv_w[:, 4 * g:4 * g + 4, :],
                             w_in_v[:, 4 * g:4 * g + 4, KV0:U0]).then_inc(mix_in[f"kv{g}"], 16)
            woa = w_o_attn[0].rearrange("(g k p) n -> g p k n", g=NKV, p=HD)
            wop = w_o_pool[0].rearrange("(k p) n -> p k n", p=P)
            wo = w_out[0].rearrange("(k p) n -> p k n", p=P)

            def wait_step(name):
                i, before_ = turn(name)
                sp.wait_ge(bank_full[i], before_ + 1)

            for i, name in enumerate(MIX):
                s, j = i % SLOTS, int(name[-1])
                if i >= SLOTS:
                    wait_step(LAST[MIX[s]])
                got = mix_in[name]
                if name[0] == "q":
                    for g in range(NKV):
                        sp.dma_start(slot(s, k=KD)[:, :, g * P:(g + 1) * P],
                                     w_in_v[:, :, g * 512 + j * P:g * 512 + (j + 1) * P]).then_inc(got, 16)
                elif name[:2] in ("u0", "u1"):
                    sp.dma_start(slot(s, k=KD), w_in_v[:, :, U0 + j * 256:U0 + (j + 1) * 256]).then_inc(got, 16)
                elif name[:2] in ("ga", "gp"):
                    c0 = (GA0 if name[1] == "a" else GP0) + j * 256
                    sp.dma_start(slot(s, k=KD), w_in_v[:, :, c0:c0 + 256]).then_inc(got, 16)
                elif name[:2] == "op":
                    sp.dma_start(slot(s, k=NG), wop[:, :, j * 512:(j + 1) * 512]).then_inc(got, 16)
                elif name[:2] == "oa":
                    for g in range(NKV):
                        sp.dma_start(ring[g * HD:(g + 1) * HD, s, :].rearrange("p (k n) -> p k n", k=KD),
                                     woa[g, :, :, j * 256:(j + 1) * 256]).then_inc(got, 16)
                else:
                    sp.dma_start(slot(s, k=2), wo[:, 2 * j:2 * j + 2, :]).then_inc(got, 16)
            sp.wait_ge(scores_ready, 2)
            sp.dma_start(ln_g, ln1_g[0].partition_broadcast(P)).then_inc(ln1_in, 16)
            sp.dma_start(ln_b, ln1_b[0].partition_broadcast(P)).then_inc(ln1_in, 16)
            wait_step("o11")
            for i in range(3):
                rows_ = slice(i * NE, (i + 1) * NE)
                sp.dma_start(bias_raw[rows_, 0:2 * D], b_gu[0]).then_inc(bias_in, 16)
                sp.dma_start(bias_raw[rows_, 2 * D:], b_down[0]).then_inc(bias_in, 16)

            gu_v = w_gu[0].rearrange("e (k p) n -> e k p n", p=P)
            dn_v = w_down[0].rearrange("e (j k p) n -> e j p k n", k=2, p=P)

            def load_chunk(e, i, dst, got):
                if i < GU_CHUNKS:
                    sp.dma_start(dst, gu_v[e, i]).then_inc(got, 16)
                else:
                    sp.dma_start(dst.rearrange("p (k n) -> p k n", k=2), dn_v[e, i - GU_CHUNKS]).then_inc(got, 16)

            def load_expert(n, e, chunks):
                for i in chunks:
                    sp.wait_ge(slot_free[i], n - 1 if i < len(annex) else n)
                    load_chunk(e, i, ring[:, i, :], slot_full[i])

            early = [i for i in range(SLOTS) if not LAST[MIX[SLOTS + i]].startswith("h")]
            for i in early:
                wait_step(LAST[MIX[SLOTS + i]])
                load_chunk(0, i, ring[:, i, :], slot_full[i])
            sp.wait_ge(probs_used, NT)
            for i in range(len(annex)):
                if i == NT:
                    sp.wait_ge(merged, 4)
                load_chunk(1, i, annex[i], annex_in[i])
            for i in range(SLOTS):
                if i not in early:
                    wait_step(LAST[MIX[SLOTS + i]])
                    load_chunk(0, i, ring[:, i, :], slot_full[i])
            load_expert(2, 2, range(len(annex)))
            load_expert(1, 1, range(len(annex), SLOTS))
            load_expert(2, 2, range(len(annex), SLOTS))
            with sp.Fori(3, NE) as e:
                load_expert(e, e, range(SLOTS))
            sp.wait_ge(flag_ready, 1)
            over = sp.value_load(most_i[0:1, 0:1], min_val=0, max_val=SEQ)
            with sp.If(over > CAP):
                with sp.Fori(1, ROUNDS) as r:
                    with sp.Fori(0, NE) as e:
                        load_expert(r * NE + e, e, range(SLOTS))
            for t in range(NT):
                sp.wait_ge(normed, NT + t + 1)
                sp.dma_start(out[0, t * P:(t + 1) * P, :], xs[:, t, :]).then_inc(out_done, 16)
            sp.wait_ge(out_done, 16 * NT)

        @block.gpsimd
        def _(pool):
            pool.memset(ident[:, :], 0.0).then_inc(consts, 1)
            pool.memset(ones[:, :], 1.0).then_inc(consts, 1)
            pool.memset(sel3[:, :], 0.0).then_inc(consts, 1)
            pool.wait_ge(consts, 3)
            pool.affine_select(out=ident[:, :], in_=ident[:, :], compare_op=ALU.not_equal, fill=1.0, base=0,
                               pattern=[[-1, P]], channel_multiplier=1).then_inc(consts, 1)
            pool.memset(vs[0:CH, 0, :], 0.0).then_inc(consts, 1)
            pool.memset(ur[:, 0:NG * (PAD + SEQ)], 0.0).then_inc(consts, 1)
            pool.memset(oT[:, :], 0.0).then_inc(consts, 1)
            pool.memset(zeros[:, :], 0.0).then_inc(consts, 1)
            pool.affine_select(out=before[:, :], in_=ones[:, :], compare_op=ALU.is_gt, fill=0.0, base=0,
                               pattern=[[1, P]], channel_multiplier=-1).then_inc(consts, 1)
            pool.iota(slot_no[:, :, :], pattern=[[0, 2], [1, CAP]], base=0, channel_multiplier=0,
                      allow_small_or_imprecise_dtypes=True).then_inc(consts, 1)
            pool.iota(inv_n[:, :], pattern=[[1, PAD]], base=1, channel_multiplier=0,
                      allow_small_or_imprecise_dtypes=True).then_inc(consts, 1)
            for i in range(3):
                pool.affine_select(out=sel3[:, :], in_=sel3[:, :], compare_op=ALU.not_equal, fill=1.0,
                                   base=-i * NE, pattern=[[-1, NE]], channel_multiplier=1).then_inc(consts, 1)
                pool.wait_ge(consts, 12 + i)
            pool.wait_ge(bias_in, 6 * 16)
            step = 0
            for i in range(3):
                for j in range(i, 3):
                    rows_ = slice(j * NE, (j + 1) * NE)
                    pool.tensor_copy(bias3[rows_, :], bias_raw[rows_, :]).then_inc(pool_step, 1)
                step += 3 - i
                pool.wait_ge(pool_step, step)
                for j in range(i + 1, 3):
                    rows_ = slice(j * NE, (j + 1) * NE)
                    pool.tensor_tensor(bias_raw[rows_, :], bias_raw[rows_, :], bias3[rows_, :],
                                       ALU.subtract).then_inc(pool_step, 1)
                step += 2 - i
                pool.wait_ge(pool_step, step)
            pool.sem_inc(bias_split, 1)
        CONSTS = 14

        @block.scalar
        def _(act):
            b = b_in[0]
            qb = b[0:D].rearrange("(g m c) -> g m c", g=NKV, c=HD)
            for g in range(NKV):
                act.dma_start(rows[0:8, g * HD:(g + 1) * HD], qb[g]).then_inc(small_in, 16)
            act.dma_start(rows[8:9, :], b[KV0:KV0 + P].rearrange("(m c) -> m c", c=P)).then_inc(small_in, 16)
            act.dma_start(rows[9:29, :], b[U0:].rearrange("(m c) -> m c", c=P)).then_inc(small_in, 16)
            act.dma_start(rows[29:33, :], pool_scale[0].rearrange("(m c) -> m c", c=P)).then_inc(small_in, 16)
            act.dma_start(bv[:, :], b[KV0 + P:U0].partition_broadcast(P)).then_inc(small_in, 16)
            act.dma_start(sink_b[:, :], sinks[0].partition_broadcast(P)).then_inc(small_in, 16)
            act.dma_start(wmix[:, :, :], w_pool_mix[0].rearrange("g c d -> c g d")).then_inc(late_in, 16)
            act.dma_start(wrt[:, :, :], w_router[0].rearrange("(k p) e -> p k e", p=P)).then_inc(late_in, 16)
            act.dma_start(br_b[:, :], b_router[0].partition_broadcast(P)).then_inc(late_in, 16)

            def full(name):
                i, before_ = turn(name)
                act.wait_ge(bank_full[i], before_ + 1)
                return bank[i]

            def free(name):
                return bank_free[turn(name)[0]]

            def turn_x(c):
                t, g = c // 2, c % 2
                ps = full(f"x{c}")
                act.activation(feat[:, 4 * g:4 * g + 4, t * P:(t + 1) * P],
                               ps[:, :].rearrange("p (k s) -> p k s", k=4), ACT.Copy).then_inc(free(f"x{c}"), 1)

            turn_x(0)
            turn_x(2)
            i, before_ = turn("v")
            act.wait_ge(bank_free[i], before_ + 1)
            act.dma_start(vs[CH:P, 0, :], vs[0:CH, 1, :]).then_inc(v_moved, 16)
            act.dma_start(vs[0:CH, 2, :], vs[CH:P, 1, :]).then_inc(v_moved, 16)
            act.dma_start(vs[CH:P, 2, :], vs[0:CH, 3, :]).then_inc(v_moved, 16)
            for j in range(4):
                ps = full(f"q{j}")
                if j == 0:
                    act.wait_ge(bank_free[turn("rows")[0]], turn("rows")[1] + 1)
                for i in range(2):
                    m = 2 * j + i
                    ins = act.activation(qT[:, m, :], ps[:, i * SEQ:(i + 1) * SEQ], ACT.Identity,
                                         bias=cols[:, m:m + 1])
                ins.then_inc(free(f"q{j}"), 1)

            for t in range(NT):
                act.wait_ge(shifted, t + 1)
                act.activation(probs[:, t, :], probs[:, t, :], ACT.Exp).then_inc(act_step, 1)
                act.activation(sden[:, t, :], sden[:, t, :], ACT.Exp).then_inc(exps_ready, 1)

            def sigmoid(a, j):
                name = f"g{'ap'[a]}{j}"
                ps = full(name)
                for i in range(2):
                    m = 2 * j + i
                    c = 13 + a * KD + m
                    ins = act.activation(gates[:, a, m, :], ps[:, i * SEQ:(i + 1) * SEQ], ACT.Sigmoid,
                                         bias=cols[:, c:c + 1])
                ins.then_inc(free(name), 1)

            def turn_probs(t):
                for c in (0, 2):
                    name = f"pt{t}{c}"
                    ps = full(name)
                    act.activation(probsT[t][:, 4 * c:4 * c + 4, :],
                                   ps[:, :].rearrange("p (h q) -> p h q", h=4), ACT.Copy).then_inc(free(name), 1)

            for j in range(4):
                sigmoid(0, j)
            turn_probs(0)
            for j in range(3):
                sigmoid(1, j)
            turn_probs(1)
            sigmoid(1, 3)

            def root(i):
                act.wait_ge(var_ready, i + 1)
                act.activation(rstd[:, i % NT, :], rstd[:, i % NT, :], ACT.Sqrt).then_inc(std_ready, 1)

            for t in range(NT):
                root(t)
            for c in (0, 2):
                t, g = c // 2, c % 2
                ps = full(f"t{c}")
                act.activation(feat[:, 4 * g:4 * g + 4, t * P:(t + 1) * P],
                               ps[:, :].rearrange("p (k s) -> p k s", k=4), ACT.Copy).then_inc(free(f"t{c}"), 1)
            act.wait_ge(normed, NT)
            act.dma_start(ln_g, ln2_g[0].partition_broadcast(P)).then_inc(ln2_in, 16)
            act.dma_start(ln_b, ln2_b[0].partition_broadcast(P)).then_inc(ln2_in, 16)
            act.wait_ge(top_shift, 1)
            act.activation(tex[:, :, :], tex[:, :, :], ACT.Exp).then_inc(top_exp, 1)

            def take_gathered(q):
                act.wait_ge(gathered, q + 1)
                for i, ps in enumerate((turn_ps, down_ps)):
                    ins = act.activation(xg[:, 4 * i:4 * i + 4, :, :],
                                         ps[:, :].rearrange("p (k i j) -> p k i j", k=4, i=2), ACT.Copy)
                ins.then_inc(xg_ready, 1)

            def take_sigmoid(n):
                act.wait_ge(gate_clamped, n + 1)
                act.activation(sig, gate_c, ACT.Sigmoid, scale=SW_ALPHA).then_inc(sig_ready, 1)

            def take_rows(n, i):
                act.wait_ge(down_done, n + 1)
                for h in range(2):
                    part = slice(CAP * (h ^ i), CAP * (h ^ i) + CAP)
                    ins = act.activation(ye[h][part, :], down_ps[part, :], ACT.Copy)
                ins.then_inc(ye_ready, 1)

            def pair(q):
                take_sigmoid(2 * q)
                take_rows(2 * q, 0)
                take_sigmoid(2 * q + 1)
                take_gathered(q + 1)
                act.wait_ge(spread_turned, q + 1)
                act.activation(spreadT, gate_ps[:, :].rearrange("p (t h q) -> p t h q", t=NT, h=2),
                               ACT.Copy).then_inc(spreadT_ready, 1)
                take_rows(2 * q + 1, 1)

            take_gathered(0)
            pair(0)
            with act.Fori(1, NE // 2) as q:
                pair(q)
            act.wait_ge(flag_ready, 1)
            over = act.value_load(most_i[0:1, 0:1], min_val=0, max_val=SEQ)
            with act.If(over > CAP):
                with act.Fori(NE // 2, ROUNDS * NE // 2) as q:
                    pair(q)
            for t in range(NT):
                root(NT + t)

        @block.tensor
        def _(pe):
            pe.wait_ge(consts, 4)

            def take(name):
                i, before_ = turn(name)
                if before_:
                    pe.wait_ge(bank_free[i], before_)
                return bank[i]

            def full(name):
                return bank_full[turn(name)[0]]

            for c in range(4):
                t, g = c // 2, c % 2
                pe.wait_ge(x_in[c], 16)
                ps = take(f"x{c}")
                for k in range(4):
                    mm = pe.transpose(ps[:, k * P:(k + 1) * P], xs[:, t, (4 * g + k) * P:(4 * g + k + 1) * P],
                                      ident[:, :])
                mm.then_inc(full(f"x{c}"), 1)
            xT = feat[:, :, :]
            ps = take("k")
            for c in range(4):
                pe.wait_ge(bank_free[turn(f"x{c}")[0]], turn(f"x{c}")[1] + 1)
            for k in range(KD):
                if k % 4 == 0:
                    pe.wait_ge(mix_in[f"kv{k // 4}"], 16)
                mm = pe.matmul(ps[:, 0:SEQ], kv_w[:, k, 0:P], xT[:, k, :], start=(k == 0), stop=(k == KD - 1))
            mm.then_inc(full("k"), 1)
            ps = take("v")
            for t in range(NT):
                for k in range(KD):
                    mm = pe.matmul(ps[:, t * P:(t + 1) * P], xT[:, k, t * P:(t + 1) * P], kv_w[:, k, P:2 * P],
                                   start=(k == 0), stop=(k == KD - 1))
            mm.then_inc(full("v"), 1)
            ps = take("rows")
            pe.wait_ge(small_in, 7 * 16)
            pe.transpose(ps[:, 0:33], rows[:, :], ident[0:33, 0:33]).then_inc(full("rows"), 1)

            def project(name, weight, rhs, ks):
                ps = take(name)
                for i in range(2):
                    for k in range(ks):
                        mm = pe.matmul(ps[:, i * SEQ:(i + 1) * SEQ], weight(k, i), rhs(k),
                                       start=(k == 0), stop=(k == ks - 1))
                mm.then_inc(full(name), 1)

            def from_x(name):
                s = MIX.index(name) % SLOTS
                if name[0] == "q":
                    pe.wait_ge(mix_in[name], 32)
                    ps = take(name)
                    for i in range(2):
                        for k in range(KD):
                            for g in range(NKV):
                                mm = pe.matmul(ps[g * HD:(g + 1) * HD, i * SEQ:(i + 1) * SEQ],
                                               slot(s, k=KD)[:, k, g * P + i * HD:g * P + (i + 1) * HD],
                                               xT[:, k, :], start=(k == 0), stop=(k == KD - 1))
                    mm.then_inc(full(name), 1)
                else:
                    pe.wait_ge(mix_in[name], 16)
                    project(name, lambda k, i: slot(s, k=KD)[:, k, i * P:(i + 1) * P],
                            lambda k: xT[:, k, :], KD)

            def score(t):
                if t == 0:
                    pe.wait_ge(mask_set, 1)
                    for name in ("k", "q0", "q1", "q2", "q3"):
                        pe.wait_ge(bank_free[turn(name)[0]], turn(name)[1] + 1)
                else:
                    pe.wait_ge(scores_read, 1)
                for m in range(KD):
                    for g in range(NKV):
                        rows_ = slice(g * HD, (g + 1) * HD)
                        for half in range(2):
                            c = 2 * t + half
                            lo = CH if c == 0 else 0
                            mm = pe.matmul(scores[half * CH:(half + 1) * CH, g * KD + m, lo:P],
                                           qT[rows_, m, c * CH:(c + 1) * CH],
                                           kT[rows_, (c - 1) * CH + lo:(c + 1) * CH], start=True, stop=True)
                mm.then_inc(scores_ready, 1)

            def turn_probs(t):
                pe.wait_ge(probs_ready, t + 1)
                for c in range(4):
                    name = f"pt{t}{c}"
                    ps = take(name)
                    for h in range(4):
                        mm = pe.transpose(ps[:, h * P:(h + 1) * P],
                                          probs[:, t, (4 * c + h) * P:(4 * c + h + 1) * P], ident[:, :])
                    mm.then_inc(full(name), 1)

            def attend(t):
                pe.wait_ge(v_moved, 3 * 16)
                for c in range(4):
                    pe.wait_ge(bank_free[turn(f"pt{t}{c}")[0]], turn(f"pt{t}{c}")[1] + 1)
                for half in range(2):
                    c = 2 * t + half
                    name = f"o{t}{half}"
                    ps = take(name)
                    for g in range(NKV):
                        mm = pe.matmul(ps[g * HD:(g + 1) * HD, :], vs[:, c, g * HD:(g + 1) * HD],
                                       probsT[t][:, g * KD:(g + 1) * KD, half * CH:(half + 1) * CH],
                                       start=True, stop=True)
                    mm.then_inc(full(name), 1)

            for j in range(4):
                from_x(f"q{j}")
            score(0)
            for name in ("u0", "u1"):
                from_x(name)
            score(1)
            for j in range(4):
                from_x(f"ga{j}")
            pe.wait_ge(late_in, 3 * 16)
            pe.wait_ge(pooled, NG)
            for j in range(2):
                ps = take(f"mix{j}")
                for i in range(2):
                    g = 2 * j + i
                    mm = pe.matmul(ps[:, i * SEQ:(i + 1) * SEQ], wmix[:, g, :], rT[:, g, :], start=True, stop=True)
                mm.then_inc(full(f"mix{j}"), 1)
            turn_probs(0)
            attend(0)
            for j in range(3):
                from_x(f"gp{j}")
            turn_probs(1)
            attend(1)
            from_x("gp3")
            for j in range(2):
                pe.wait_ge(bank_free[turn(f"mix{j}")[0]], turn(f"mix{j}")[1] + 1)
            for j in range(4):
                s = MIX.index(f"op{j // 2}") % SLOTS
                pe.wait_ge(mix_in[f"op{j // 2}"], 16)
                project(f"yp{j}",
                        lambda k, i: slot(s, k=NG)[:, k, (j % 2) * 256 + i * P:(j % 2) * 256 + (i + 1) * P],
                        lambda k: uT[:, k, PAD:PAD + SEQ], NG)
            for t in range(NT):
                for half in range(2):
                    pe.wait_ge(bank_free[turn(f"o{t}{half}")[0]], turn(f"o{t}{half}")[1] + 1)
            for j in range(4):
                s = MIX.index(f"oa{j}") % SLOTS
                pe.wait_ge(mix_in[f"oa{j}"], 32)
                project(f"ya{j}", lambda k, i: slot(s, k=KD)[:, k, i * P:(i + 1) * P],
                        lambda k: o_heads[:, k, :], KD)
            pe.wait_ge(merged, 4)
            for j in range(4):
                pe.wait_ge(mix_in[f"wo{j}"], 16)
            for t in range(NT):
                for half in range(2):
                    name = f"h{t}{half}"
                    ps = take(name)
                    for k in range(KD):
                        s = MIX.index(f"wo{k // 2}") % SLOTS
                        mm = pe.matmul(ps[:, :], feat[:, k, t * P:(t + 1) * P],
                                       slot(s, k=2)[:, k % 2, half * 512:(half + 1) * 512],
                                       start=(k == 0), stop=(k == KD - 1))
                    mm.then_inc(full(name), 1)
            for t in range(NT):
                pe.wait_ge(normed, t + 1)
                for c in (2 * t, 2 * t + 1):
                    ps = take(f"t{c}")
                    for k in range(4):
                        kk = 4 * (c % 2) + k
                        mm = pe.transpose(ps[:, k * P:(k + 1) * P], xs[:, t, kk * P:(kk + 1) * P], ident[:, :])
                    mm.then_inc(full(f"t{c}"), 1)
                ps = take(f"logits{t}")
                for c in (2 * t, 2 * t + 1):
                    pe.wait_ge(bank_free[turn(f"t{c}")[0]], turn(f"t{c}")[1] + 1)
                for k in range(KD):
                    mm = pe.matmul(ps[:, 0:NE], feat[:, k, t * P:(t + 1) * P], wrt[:, k, :],
                                   start=(k == 0), stop=(k == KD - 1))
                mm.then_inc(full(f"logits{t}"), 1)
            for i in range(4):
                pe.matmul(wide[:, i, :], zeros[:, 0:P], zeros[:, :], start=True, stop=False, skip_group_check=True)
            ps = take("rank")
            pe.wait_ge(chosen_ready, 1)
            pe.matmul(ps[:, 0:NE], before[:, :], chosen[:, 0, :], start=True, stop=True)
            pe.matmul(ps[:, NE:2 * NE], ones[:, :], chosen[:, 0, :], start=True, stop=False)
            pe.matmul(ps[:, NE:2 * NE], before[:, :], chosen[:, 1, :], start=False, stop=True)
            pe.matmul(ps[:, 2 * NE:3 * NE], ones[:, :], chosen[:, 0, :], start=True, stop=False)
            pe.matmul(ps[:, 2 * NE:3 * NE], ones[:, :], chosen[:, 1, :], start=False,
                      stop=True).then_inc(full("rank"), 1)

            def gather(q):
                pe.wait_ge(pick_ready, q + 1)
                for k in range(KD):
                    for t in range(NT):
                        mm = pe.matmul((turn_ps, down_ps)[k // 4][:, (k % 4) * P:(k % 4 + 1) * P],
                                       xs[:, t, k * P:(k + 1) * P], pick[:, t, :, :],
                                       start=(t == 0), stop=(t == NT - 1))
                mm.then_inc(gathered, 1)

            def combine(t, stop):
                for half in range(2):
                    mm = pe.matmul(wide[:, 2 * t + half, :], spreadT[:, t, half, :], ye[half],
                                   start=False, stop=stop, skip_group_check=True)
                return mm

            def gate_up(n, i, spot):
                for k in range(GU_CHUNKS):
                    w, got, count = spot(k)
                    pe.wait_ge(got, count)
                    for c, ps in enumerate((gate_ps, up_ps)):
                        for half in range(2):
                            col = (2 * c + half) * 512
                            mm = pe.matmul(ps[half * CAP:(half + 1) * CAP, :], xg[:, k, i, :], w[:, col:col + 512],
                                           start=(k == 0), stop=False)
                    if got is slot_full[k]:
                        mm.then_inc(slot_free[k], 1)
                for c, ps in enumerate((gate_ps, up_ps)):
                    for half in range(2):
                        col = (2 * c + half) * 512
                        mm = pe.matmul(ps[half * CAP:(half + 1) * CAP, :], one_e[:, i, :],
                                       bias3[:, col:col + 512], start=False, stop=True)
                mm.then_inc(gu_done, 1)

            def turn_act(n):
                pe.wait_ge(act_ready, n + 1)
                for f in range(4):
                    mm = pe.transpose(turn_ps[:, f * P:(f + 1) * P], act_v[:, f * P:(f + 1) * P], ident[:, :])
                mm.then_inc(act_turned, 1)

            def down(n, i, spot):
                pe.wait_ge(actT_ready, n + 1)
                pe.wait_ge(ye_ready, n + 1)
                for k in range(KD):
                    c = GU_CHUNKS + k // 2
                    w, got, count = spot(c)
                    if k % 2 == 0:
                        pe.wait_ge(got, count)
                    for half in range(2):
                        part = CAP * (half ^ i)
                        mm = pe.matmul(down_ps[part:part + CAP, :], actT[:, k % 4, k // 4, :],
                                       w[:, (k % 2) * D + half * 512:(k % 2) * D + (half + 1) * 512],
                                       start=(k == 0), stop=False)
                    if k % 2:
                        mm.then_inc(slot_free[c], 1)
                for half in range(2):
                    part = CAP * (half ^ i)
                    mm = pe.matmul(down_ps[part:part + CAP, :], one_e[:, i, :],
                                   bias3[:, 2 * D + half * 512:2 * D + (half + 1) * 512], start=False, stop=True)
                mm.then_inc(down_done, 1)

            def in_ring(n):
                return lambda c: (ring[:, c, :], slot_full[c], 16 * (n if c < len(annex) else n + 1))

            def pair(q, first, second):
                n = 2 * q
                pe.wait_ge(xg_ready, q + 1)
                pe.wait_ge(spreadT_ready, q + 1)
                pe.wait_ge(one_ready, q + 1)
                gate_up(n, 0, first)
                pe.wait_ge(ye_ready, n + 1)
                for t in range(NT):
                    mm = combine(t, False)
                mm.then_inc(combined, 1)
                turn_act(n)
                down(n, 0, first)
                gate_up(n + 1, 1, second)
                pe.wait_ge(ye_ready, n + 2)
                gather(q + 1)
                pe.wait_ge(xg_ready, q + 2)
                turn_act(n + 1)
                pe.wait_ge(spread_ready, q + 1)
                for t in range(NT):
                    for h in range(2):
                        mm = pe.transpose(gate_ps[:, (2 * t + h) * P:(2 * t + h + 1) * P],
                                          spread[:, t, h:h + 2, :].rearrange("p i j -> p (i j)"), ident[:, :])
                mm.then_inc(spread_turned, 1)
                down(n + 1, 1, second)

            gather(0)
            pair(0, lambda c: (ring[:, c, :], slot_full[c], 16),
                 lambda c: (annex[c], annex_in[c], 16) if c < len(annex) else (ring[:, c, :], slot_full[c], 32))
            with pe.Fori(1, NE // 2) as q:
                pair(q, in_ring(2 * q), in_ring(2 * q + 1))
            pe.wait_ge(flag_ready, 1)
            over = pe.value_load(most_i[0:1, 0:1], min_val=0, max_val=SEQ)
            with pe.If(over > CAP):
                with pe.Fori(NE // 2, ROUNDS * NE // 2) as q:
                    pair(q, in_ring(2 * q), in_ring(2 * q + 1))
                pe.wait_ge(ye_ready, ROUNDS * NE + 1)
            pe.wait_ge(ye_ready, NE + 1)
            for t in range(NT):
                combine(t, True).then_inc(moe_done, 1)

        @block.vector
        def _(dve):
            done = [0]

            def then(ins):
                done[0] += 1
                ins.then_inc(dve_step, 1)
                dve.wait_ge(dve_step, done[0])

            def full(name):
                i, before_ = turn(name)
                dve.wait_ge(bank_full[i], before_ + 1)
                return bank[i]

            def free(name):
                return bank_free[turn(name)[0]]

            dve.memset(scores[0:CH, :, 0:CH], NEG).then_inc(mask_set, 1)
            for c in (1, 3):
                t, g = c // 2, c % 2
                ps = full(f"x{c}")
                dve.tensor_copy(feat[:, 4 * g:4 * g + 4, t * P:(t + 1) * P],
                                ps[:, :].rearrange("p (k s) -> p k s", k=4)).then_inc(free(f"x{c}"), 1)
            dve.wait_ge(consts, CONSTS)
            then(dve.reciprocal(inv_n[:, :], inv_n[:, :]))
            dve.wait_ge(small_in, 7 * 16)
            ps = full("v")
            dve.tensor_tensor(vs[:, 1::2, :], ps[:, 0:2 * P].rearrange("p (c n) -> p c n", c=2),
                              bv[:, :].unsqueeze(1).to_broadcast([P, 2, P]), ALU.add).then_inc(free("v"), 1)
            ps = full("rows")
            dve.tensor_copy(cols[:, :], ps[:, 0:33]).then_inc(free("rows"), 1)
            dve.wait_ge(free("rows"), turn("rows")[1] + 1)
            ps = full("k")
            dve.tensor_scalar(kT[:, :], ps[:, 0:SEQ], cols[:, 8:9], None, ALU.add).then_inc(free("k"), 1)

            def softmax_shift(t):
                dve.wait_ge(scores_ready, t + 1)
                then(dve.tensor_reduce(smax[:, t, :], scores, AX.X, ALU.max))
                then(dve.scalar_tensor_tensor(out=smax[:, t, :], in0=smax[:, t, :], scalar=HD ** -0.5,
                                              in1=sink_b[:, :], op0=ALU.mult, op1=ALU.max))
                dve.tensor_tensor(sden[:, t, :], sink_b[:, :], smax[:, t, :], ALU.subtract).then_inc(dve_step, 1)
                done[0] += 1
                then(dve.scalar_tensor_tensor(out=probs[:, t, :].rearrange("p (h k) -> p h k", h=NH), in0=scores,
                                              scalar=HD ** -0.5,
                                              in1=smax[:, t, :].unsqueeze(2).to_broadcast([P, NH, P]),
                                              op0=ALU.mult, op1=ALU.subtract))
                dve.sem_inc(scores_read, 1)
                dve.sem_inc(shifted, 1)

            def softmax_norm(t):
                p3 = probs[:, t, :].rearrange("p (h k) -> p h k", h=NH)
                dve.wait_ge(act_step, t + 1)
                dve.wait_ge(exps_ready, t + 1)
                then(dve.tensor_reduce(ssum[:, t, :], p3, AX.X, ALU.add))
                then(dve.tensor_tensor(sden[:, t, :], sden[:, t, :], ssum[:, t, :], ALU.add))
                then(dve.reciprocal(sden[:, t, :], sden[:, t, :]))
                dve.tensor_tensor(p3, p3, sden[:, t, :].unsqueeze(2).to_broadcast([P, NH, P]),
                                  ALU.mult).then_inc(probs_ready, 1)

            softmax_shift(0)
            for j in range(2):
                ps = full(f"u{j}")
                for i in range(2):
                    g = 2 * j + i
                    ins = dve.tensor_scalar(uT[:, g, PAD:], ps[:, i * SEQ:(i + 1) * SEQ], cols[:, 9 + g:10 + g],
                                            None, ALU.add)
                ins.then_inc(free(f"u{j}"), 1)
            dve.wait_ge(free("u1"), turn("u1")[1] + 1)
            softmax_shift(1)
            softmax_norm(0)
            src = uT
            for step in range(NG):
                w = 1 << step
                dst = sums[step % 2]
                then(dve.tensor_tensor(dst[:, step:, PAD:], src[:, step:, PAD:], src[:, step:, PAD - w:PAD + SEQ - w],
                                       ALU.add))
                src = dst
            for g in range(NG):
                w = 2 << g
                s = sums[g % 2]
                then(dve.scalar_tensor_tensor(out=rT[:, g, :], in0=s[:, g, PAD:], scalar=1.0 / w,
                                              in1=uT[:, g, PAD:], op0=ALU.mult, op1=ALU.subtract))
                then(dve.tensor_tensor(s[:, g, PAD:PAD + w - 1], s[:, g, PAD:PAD + w - 1], inv_n[:, 0:w - 1],
                                       ALU.mult))
                dve.tensor_tensor(rT[:, g, 0:w - 1], s[:, g, PAD:PAD + w - 1], uT[:, g, PAD:PAD + w - 1],
                                  ALU.subtract).then_inc(pooled, 1)
            dve.wait_ge(pooled, NG)
            softmax_norm(1)
            for j in range(2):
                ps = full(f"mix{j}")
                for i in range(2):
                    g = 2 * j + i
                    ins = dve.tensor_scalar(uT[:, g, PAD:], ps[:, i * SEQ:(i + 1) * SEQ], cols[:, 29 + g:30 + g],
                                            None, ALU.mult)
                ins.then_inc(free(f"mix{j}"), 1)

            def turn_probs(t):
                for c in (1, 3):
                    name = f"pt{t}{c}"
                    ps = full(name)
                    dve.tensor_copy(probsT[t][:, 4 * c:4 * c + 4, :],
                                    ps[:, :].rearrange("p (h q) -> p h q", h=4)).then_inc(free(name), 1)
                    if c == 3:
                        dve.sem_inc(probs_used, 1)

            def take_attended(t):
                for half in range(2):
                    c = 2 * t + half
                    name = f"o{t}{half}"
                    ps = full(name)
                    dve.tensor_copy(o_heads[:, :, c * CH:(c + 1) * CH],
                                    ps[:, :].rearrange("p (m q) -> p m q", m=KD)).then_inc(free(name), 1)

            for t in range(NT):
                turn_probs(t)
                take_attended(t)

            for a, branch in ((1, "yp"), (0, "ya")):
                for j in range(4):
                    name = f"{branch}{j}"
                    ps = full(name)
                    gname = f"g{'ap'[a]}{j}"
                    dve.wait_ge(free(gname), turn(gname)[1] + 1)
                    g = gates[:, a, 2 * j:2 * j + 2, :]
                    dve.tensor_tensor(g, g, ps[:, :].rearrange("p (i s) -> p i s", i=2),
                                      ALU.mult).then_inc(free(name), 1)
                    if a == 0:
                        dve.wait_ge(free(name), turn(name)[1] + 1)
                        dve.tensor_tensor(feat[:, 2 * j:2 * j + 2, :], g, gates[:, 1, 2 * j:2 * j + 2, :],
                                          ALU.add).then_inc(merged, 1)

            def layer_norm(t, i, parts, vectors_in):
                for half in range(2):
                    z = xs[:, t, half * 512:(half + 1) * 512]
                    ps, freed = parts(half)
                    ins = dve.scalar_tensor_tensor(out=z, in0=z, scalar=ALPHA, in1=ps, op0=ALU.mult, op1=ALU.add)
                    then(ins)
                    if freed is not None:
                        dve.sem_inc(freed, 1)
                    then(dve.bn_stats(stats[:, t, half, :], z))
                then(dve.bn_aggr(mv[:, t, :], stats[:, t, :, :]))
                dve.tensor_scalar(rstd[:, t, :], mv[:, t, 1:2], EPS, None, ALU.add).then_inc(var_ready, 1)
                z = xs[:, t, :]
                dve.wait_ge(vectors_in, 32)
                then(dve.scalar_tensor_tensor(out=z, in0=z, scalar=mv[:, t, 0:1], in1=ln_g, op0=ALU.subtract,
                                              op1=ALU.mult))
                dve.wait_ge(std_ready, i + 1)
                then(dve.reciprocal(rstd[:, t, :], rstd[:, t, :]))
                dve.scalar_tensor_tensor(out=z, in0=z, scalar=rstd[:, t, :], in1=ln_b, op0=ALU.mult,
                                         op1=ALU.add).then_inc(normed, 1)

            for t in range(NT):
                layer_norm(t, t, lambda half: (full(f"h{t}{half}")[:, :], free(f"h{t}{half}")), ln1_in)
                c = 2 * t + 1
                ps = full(f"t{c}")
                dve.tensor_copy(feat[:, 4:8, t * P:(t + 1) * P],
                                ps[:, :].rearrange("p (k s) -> p k s", k=4)).then_inc(free(f"t{c}"), 1)

            dve.wait_ge(late_in, 3 * 16)
            expert_no = slot_no[:, 0, 0:NE]
            for t in range(NT):
                ps = full(f"logits{t}")
                dve.tensor_tensor(logit[:, t, :], ps[:, 0:NE], br_b[:, :], ALU.add).then_inc(free(f"logits{t}"), 1)
                dve.wait_ge(free(f"logits{t}"), turn(f"logits{t}")[1] + 1)
                then(dve.max(top[:, t, :], logit[:, t, :]))
                then(dve.max_index(topi[:, t, :], top[:, t, :], logit[:, t, :]))
            then(dve.tensor_copy(topf[:, :, :], topi[:, :, 0:TOPK]))
            then(dve.tensor_tensor(hit.rearrange("p t s e -> p (t s) e"),
                                   expert_no.unsqueeze(1).to_broadcast([P, NT * TOPK, NE]),
                                   topf[:, :, :].rearrange("p t s -> p (t s)").unsqueeze(2)
                                   .to_broadcast([P, NT * TOPK, NE]), ALU.is_equal))
            then(dve.tensor_reduce(rank1[:, :, :], hit.rearrange("p t s e -> p t e s"), AX.X, ALU.add))
            dve.tensor_copy(chosen[:, :, :], rank1[:, :, :]).then_inc(chosen_ready, 1)
            dve.tensor_tensor(tex[:, :, :], top[:, :, 0:TOPK], top[:, :, 0:1].to_broadcast([P, NT, TOPK]),
                              ALU.subtract).then_inc(top_shift, 1)
            ps = full("rank")
            then(dve.scalar_tensor_tensor(out=rank1[:, :, :],
                                          in0=ps[:, 0:NT * NE].rearrange("p (t e) -> p t e", t=NT), scalar=1.0,
                                          in1=rank1[:, :, :], op0=ALU.add, op1=ALU.mult))
            then(dve.tensor_scalar(rank_n[:, :, 0:NE], rank1[:, :, :], 1.0, None, ALU.subtract))

            def pick_pair(q):
                for t in range(NT):
                    for i in range(2):
                        ins = dve.tensor_scalar(pick[:, t, i, :], slot_no[:, 0, :],
                                                rank_n[:, t, bass.ds(2 * q + i, 1)], None, ALU.is_equal)
                ins.then_inc(pick_ready, 1)

            dve.wait_ge(bias_split, 1)
            pick_pair(0)
            then(dve.tensor_reduce(most[:, :], ps[:, NT * NE:(NT + 1) * NE], AX.X, ALU.max))
            dve.tensor_copy(most_i[:, :], most[:, :]).then_inc(flag_ready, 1)
            then(dve.memset(rank_n[:, :, ROUNDS * NE:], -1.0))
            for r in range(1, ROUNDS):
                then(dve.tensor_scalar(rank_n[:, :, r * NE:(r + 1) * NE], rank1[:, :, :], 1.0 + r * CAP, None,
                                       ALU.subtract))
            dve.wait_ge(top_exp, 1)
            then(dve.tensor_reduce(tsum[:, :], tex[:, :, :], AX.X, ALU.add))
            then(dve.reciprocal(tsum[:, :], tsum[:, :]))
            then(dve.tensor_tensor(tex[:, :, :], tex[:, :, :], tsum[:, :].unsqueeze(2).to_broadcast([P, NT, TOPK]),
                                   ALU.mult))
            then(dve.tensor_tensor(hitg.rearrange("p t s e -> p (t s) e"), hit.rearrange("p t s e -> p (t s) e"),
                                   tex[:, :, :].rearrange("p t s -> p (t s)").unsqueeze(2)
                                   .to_broadcast([P, NT * TOPK, NE]), ALU.mult))
            then(dve.tensor_reduce(gate1[:, :, :], hitg.rearrange("p t s e -> p t e s"), AX.X, ALU.add))
            for r in range(ROUNDS):
                then(dve.tensor_copy(gate_n[:, :, r * NE:(r + 1) * NE], gate1[:, :, :]))
            for h in range(2):
                dve.memset(ye[h], 0.0).then_inc(zeros_ready, 1)
            dve.memset(spreadT, 0.0).then_inc(zeros_ready, 1)
            dve.wait_ge(zeros_ready, 3)
            dve.sem_inc(ye_ready, 1)
            dve.sem_inc(spreadT_ready, 1)

            def swiglu(n):
                dve.wait_ge(gu_done, n + 1)
                dve.tensor_scalar(gate_c, gate_ps[:, :], SW_LIMIT, None, ALU.min).then_inc(gate_clamped, 1)
                dve.tensor_scalar(up_c, up_ps[:, :], -SW_LIMIT, SW_LIMIT, ALU.max, ALU.min).then_inc(up_clamped, 1)
                dve.wait_ge(gate_clamped, n + 1)
                dve.wait_ge(up_clamped, n + 1)
                dve.scalar_tensor_tensor(out=up_c, in0=up_c, scalar=1.0, in1=gate_c, op0=ALU.add,
                                         op1=ALU.mult).then_inc(gated, 1)
                dve.wait_ge(gated, n + 1)
                dve.wait_ge(sig_ready, n + 1)
                dve.tensor_tensor(act_v, up_c, sig, ALU.mult).then_inc(act_ready, 1)
                dve.wait_ge(act_turned, n + 1)
                dve.tensor_copy(actT, turn_ps[:, :].rearrange("p (f h j) -> p f h j", f=4, h=2)).then_inc(actT_ready, 1)

            def pair(q, e):
                dve.wait_ge(down_done, 2 * q)
                for i in range(2):
                    ins = dve.tensor_copy(one_e[:, i, :], sel3[:, bass.ds(e + i, 1)].to_broadcast([3 * NE, CAP]))
                ins.then_inc(one_ready, 1)
                dve.wait_ge(gathered, q + 1)
                pick_pair(q + 1)
                dve.wait_ge(spread_turned, q)
                for t in range(NT):
                    for i in range(2):
                        ins = dve.tensor_scalar(spread[:, t, i::2, :], slot_no[:, 0:2 - i, :],
                                                rank_n[:, t, bass.ds(2 * q + i, 1)],
                                                gate_n[:, t, bass.ds(2 * q + i, 1)], ALU.is_equal, ALU.mult)
                ins.then_inc(spread_ready, 1)
                swiglu(2 * q)
                swiglu(2 * q + 1)

            pair(0, 0)
            with dve.Fori(1, NE // 2) as q:
                pair(q, 2 * q)
            dve.wait_ge(flag_ready, 1)
            over = dve.value_load(most_i[0:1, 0:1], min_val=0, max_val=SEQ)
            with dve.If(over > CAP):
                with dve.Fori(1, ROUNDS) as r:
                    with dve.Fori(0, NE // 2) as m:
                        pair(r * (NE // 2) + m, 2 * m)
            for t in range(NT):
                dve.wait_ge(moe_done, t + 1)
                layer_norm(t, NT + t, lambda half: (wide[:, 2 * t + half, :], None), ln2_in)


INS = ["x", "w_in", "b_in", "sinks", "w_o_attn", "w_pool_mix", "pool_scale", "w_o_pool", "w_out", "ln1_g", "ln1_b",
       "w_router", "b_router", "w_gu", "b_gu", "w_down", "b_down", "ln2_g", "ln2_b"]


def kernel(**inputs):
    import numpy as np
    import concourse.bacc as bacc
    from concourse.bass_utils import run_bass_kernel_spmd

    nc = bacc.Bacc("TRN2", target_bir_lowering=False, num_devices=1)
    arrays, args = {}, []
    for name in INS:
        a = np.ascontiguousarray(inputs[name])
        arrays[f"in_{name}_dram"] = a
        args.append(nc.dram_tensor(f"in_{name}_dram", a.shape, mybir.dt.from_np(a.dtype), kind="ExternalInput").ap())
    args.append(nc.dram_tensor("out_dram", (1, SEQ, D), F32, kind="ExternalOutput").ap())
    build_layer(nc, *args)
    r = run_bass_kernel_spmd(nc, [arrays], core_ids=[0])
    return r.results[0]["out_dram"]
```

```python
from contextlib import ExitStack

import concourse.bass as bass
from concourse import mybir

F32 = mybir.dt.float32
BF16 = mybir.dt.bfloat16
I32 = mybir.dt.int32
U32 = mybir.dt.uint32
ALU = mybir.AluOpType
ACT = mybir.ActivationFunctionType
AX = mybir.AxisListType

P = 128
D = 1024
SEQ = 256
NT = SEQ // P
KD = D // P
CH = 64
HD = 64
NH = D // HD
NKV = 2
HG = NH // NKV // 2
NG = 4
PAD = 16
NE = 32
TOPK = 4
F = D
CAP = 64
ROUNDS = SEQ // CAP
SLOTS = 12
GU_CHUNKS = KD
DN_CHUNKS = KD // 2
SLOT = 2 * D
ALPHA = 2 ** 0.25
EPS = 1e-5
NEG = -1e30
SW_ALPHA = 1.702
SW_LIMIT = 7.0
KV0 = D
U0 = KV0 + 2 * NKV * HD
GA0 = U0 + NG * P
GP0 = GA0 + D

TURNS = (["x0", "x1", "x2", "x3", "k", "v", "rows", "q0", "q1", "q2", "q3", "u0", "u1", "ga0"]
         + ["ga1", "ga2", "ga3", "mix0", "mix1"]
         + ["pt00", "pt01", "pt02", "pt03", "gp0", "o00", "o01", "gp1"]
         + ["pt10", "pt11", "pt12", "pt13", "gp2", "o10", "o11", "gp3"]
         + ["yp0", "yp1", "yp2", "yp3", "ya0", "ya1", "ya2", "ya3"]
         + ["h00", "h01", "h10", "h11", "t0", "t1", "logits0", "t2", "t3", "logits1", "rank1"])
assert len(TURNS) % 4 == 2


def turn(name):
    t = TURNS.index(name)
    return t % 4, t // 4


def build_layer(nc, x, w_in, b_in, sinks, w_o_attn, w_pool_mix, pool_scale, w_o_pool, w_out, ln1_g, ln1_b,
                w_router, b_router, w_gu, b_gu, w_down, b_down, ln2_g, ln2_b, out):
    ctx = ExitStack()
    with ctx:
        def sb(name, shape, dt=F32):
            return ctx.enter_context(nc.sbuf_tensor(name, shape, dt))

        def sem(name):
            return ctx.enter_context(nc.semaphore(name))

        ring = sb("ring", [P, SLOTS, SLOT])
        xs = sb("xs", [P, NT, D])
        feat = sb("feat", [P, KD, SEQ])
        qln = sb("qln", [P, 2 * D])
        small = sb("small", [P, SLOT])
        ur = sb("ur", [P, NG * (PAD + 2 * SEQ)])
        gates = sb("gates", [P, 2, KD, SEQ])
        probs = sb("probs", [P, NT, NH * P])
        work = sb("work", [P, 2 * NH * P])
        bias3 = sb("bias3", [3 * NE, 3 * D], BF16)
        sel3 = sb("sel3", [3 * NE, NE], BF16)
        one_e = sb("one_e", [3 * NE, 2, CAP], BF16)
        oT = sb("oT", [P, 2 * NG * (PAD + SEQ)])
        ident = sb("ident", [P, P])
        before = sb("before", [P, P], BF16)
        ones = sb("ones", [P, P], BF16)
        slot_no = sb("slot_no", [P, 2, CAP])
        zeros = sb("zeros", [P, 512], BF16)
        wrt = sb("wrt", [P, KD, NE])
        cols = sb("cols", [P, 33])
        sink_b = sb("sink_b", [P, NH])
        br_col = sb("br_col", [NE, 1])
        inv_n = sb("inv_n", [P, PAD])
        smax = sb("smax", [P, NT, NH])
        ssum = sb("ssum", [P, NT, NH])
        sden = sb("sden", [P, NT, NH])
        stats = sb("stats", [P, NT, 2, 6])
        mv = sb("mv", [P, NT, 2])
        rstd = sb("rstd", [P, NT, 1])
        shift = sb("shift", [P, 1])
        logitT = sb("logitT", [NE, NT, P])
        top = sb("top", [P, NT, 8])
        topi = sb("topi", [P, NT, 8], U32)
        topf = sb("topf", [P, NT, TOPK])
        tex = sb("tex", [P, NT, TOPK])
        tsum = sb("tsum", [P, NT])
        chosen = sb("chosen", [P, NT, NE], BF16)
        gate1 = sb("gate1", [P, NT, NE])
        rank1 = sb("rank1", [P, NT, NE])
        rank_n = sb("rank_n", [P, NT, ROUNDS * NE + 2])
        gate_n = sb("gate_n", [P, NT, ROUNDS * NE])
        most = sb("most", [P, 1])
        most_i = sb("most_i", [P, 1], I32)

        qT = qln[:, :].rearrange("p (m s) -> p m s", m=KD)
        halves = (slice(0, 512), slice(512, D))
        ln_g, ln_b = qln[:, 0:D], qln[:, D:2 * D]
        uT = ur[:, 0:NG * (PAD + SEQ)].rearrange("p (g s) -> p g s", g=NG)
        rT = ur[:, NG * (PAD + SEQ):].rearrange("p (g s) -> p g s", g=NG)
        wmix = small[:, 0:512].rearrange("p (g n) -> p g n", g=NG)
        vs = small[:, 512:1024].rearrange("p (c n) -> p c n", c=4)
        kT = small[:, 1024:1536].rearrange("p (i s) -> p i s", i=NKV)
        bv = small[:, 1536:1664]
        rows = small[0:33, 1664:1792]
        sums = [oT[:, i * NG * (PAD + SEQ):(i + 1) * NG * (PAD + SEQ)].rearrange("p (g s) -> p g s", g=NG)
                for i in range(2)]
        o_heads = oT[:, 0:KD * SEQ].rearrange("p (m s) -> p m s", m=KD)
        kv_w = work[:, 0:SLOT].rearrange("p (k n) -> p k n", k=KD)
        probsT = [work[:, t * NH * P:(t + 1) * NH * P].rearrange("p (h q) -> p h q", h=NH) for t in range(NT)]
        bias_raw = work[0:3 * NE, 0:3 * D]
        xg = work[:, 0:1024].rearrange("p (k i j) -> p k i j", k=KD, i=2)
        gate_c = work[:, 1024:1536]
        up_c = work[:, 1536:2048]
        sig = work[:, 2048:2560]
        actT = work[:, 2560:3072].rearrange("p (f h j) -> p f h j", f=4, h=2)
        spreadT = work[:, 3072:3584].rearrange("p (t h q) -> p t h q", t=NT, h=2)
        flat = feat[:, :, :].rearrange("p k s -> p (k s)")
        ye = [flat[:, h * 512:(h + 1) * 512] for h in range(2)]
        pick = work[:, 3840:4096].rearrange("p (t i j) -> p t i j", t=NT, i=2)
        spread = flat[:, 1024:1408].rearrange("p (t i j) -> p t i j", t=NT, i=3)
        hit, hitg = [a.rearrange("p (t s e) -> p t s e", t=NT, s=TOPK)
                     for a in (work[:, 3584:3840], flat[:, 1408:1664])]
        annex = ([probs[:, t, :] for t in range(NT)] + [small[:, :], ur[:, 0:SLOT], oT[:, 0:SLOT]]
                 + [gates[:, a, :, :].rearrange("p k s -> p (k s)") for a in range(2)] + [qln[:, :]])

        wide = ctx.enter_context(nc.psum_tensor("wide", [P, 4, 512], F32))
        bank = [ctx.enter_context(nc.psum_tensor(f"bank{i}", [P, 512], F32)) for i in range(4)]
        scores = wide[:, :, :].rearrange("p b (h k) -> p (b h) k", k=P)
        gate_ps, up_ps, down_ps, turn_ps = bank
        logit_ps = [bank[turn(f"logits{t}")[0]][:, P:P + NE] for t in range(NT)]
        rank0_ps = bank[turn("logits0")[0]][:, NE:2 * NE]

        consts = sem("consts")
        x_in = [sem(f"x_in{c}") for c in range(4)]
        small_in = sem("small_in")
        late_in = sem("late_in")
        mix_in = {}
        bank_full = [sem(f"bank_full{i}") for i in range(4)]
        bank_free = [sem(f"bank_free{i}") for i in range(4)]
        mask_set = sem("mask_set")
        scores_ready = sem("scores_ready")
        scores_read = sem("scores_read")
        shifted = sem("shifted")
        exps_ready = sem("exps_ready")
        probs_ready = sem("probs_ready")
        pooled = sem("pooled")
        merged = sem("merged")
        var_ready = sem("var_ready")
        std_ready = sem("std_ready")
        scale_ready = sem("scale_ready")
        pool_normed = sem("pool_normed")
        act_normed = sem("act_normed")
        scaled = sem("scaled")
        normed = sem("normed")
        ln1_in = sem("ln1_in")
        ln2_in = sem("ln2_in")
        v_moved = sem("v_moved")
        bias_in = sem("bias_in")
        pool_step = sem("pool_step")
        bias_split = sem("bias_split")
        k_moved = sem("k_moved")
        logitT_ready = sem("logitT_ready")
        logit_turned = sem("logit_turned")
        pick_first = sem("pick_first")
        rank0_done = sem("rank0_done")
        top_shift = sem("top_shift")
        top_exp = sem("top_exp")
        chosen_ready = sem("chosen_ready")
        flag_ready = sem("flag_ready")
        zeros_ready = sem("zeros_ready")
        dve_step = sem("dve_step")
        act_step = sem("act_step")
        slot_free = [sem(f"slot_free{i}") for i in range(SLOTS)]
        slot_full = [sem(f"slot_full{i}") for i in range(SLOTS)]
        annex_free = [sem(f"annex_free{i}") for i in range(len(annex))]
        annex_full = [sem(f"annex_full{i}") for i in range(len(annex))]
        pick_ready = sem("pick_ready")
        spread_ready = sem("spread_ready")
        one_ready = sem("one_ready")
        gathered = sem("gathered")
        xg_ready = sem("xg_ready")
        gate_done = sem("gate_done")
        up_done = sem("up_done")
        gate_clamped = sem("gate_clamped")
        up_clamped = sem("up_clamped")
        gated = sem("gated")
        sig_ready = sem("sig_ready")
        act_ready = sem("act_ready")
        act_turned = sem("act_turned")
        actT_ready = sem("actT_ready")
        spread_turned = sem("spread_turned")
        spreadT_ready = sem("spreadT_ready")
        down_done = sem("down_done")
        ye_ready = sem("ye_ready")
        ye2_ready = sem("ye2_ready")
        moe_done = sem("moe_done")
        out_done = sem("out_done")

        w_in_v = w_in[0].rearrange("(k p) n -> p k n", p=P)

        def slot(i, **kw):
            return ring[:, i, :].rearrange("p (k n) -> p k n", **kw)

        MIX = ([f"q{j}" for j in range(4)] + ["u0", "u1"] + [f"ga{j}" for j in range(4)]
               + [f"gp{j}" for j in range(4)] + ["op0", "op1"] + [f"oa{j}" for j in range(4)]
               + [f"wo{j}" for j in range(4)])
        assert len(MIX) == 2 * SLOTS
        LAST = {name: {"op": f"yp{2 * int(name[-1]) + 1}", "oa": f"ya{name[-1]}", "wo": "h11"}.get(name[:2], name)
                for name in MIX}
        for name in MIX + ["kv0", "kv1"]:
            mix_in[name] = sem(f"in_{name}")

        block = ctx.enter_context(nc.Block())

        @block.sync
        def _(sp):
            for c in range(4):
                t, g = c // 2, c % 2
                sp.dma_start(xs[:, t, g * 512:(g + 1) * 512],
                             x[0, t * P:(t + 1) * P, g * 512:(g + 1) * 512]).then_inc(x_in[c], 16)
            for g in range(2):
                sp.dma_start(kv_w[:, 4 * g:4 * g + 4, :],
                             w_in_v[:, 4 * g:4 * g + 4, KV0:U0]).then_inc(mix_in[f"kv{g}"], 16)
            b = b_in[0]
            sp.dma_start(rows[0:9, :], b[0:KV0 + P].rearrange("(m c) -> m c", c=P)).then_inc(small_in, 16)
            sp.dma_start(rows[9:29, :], b[U0:].rearrange("(m c) -> m c", c=P)).then_inc(small_in, 16)
            sp.dma_start(rows[29:33, :], pool_scale[0].rearrange("(m c) -> m c", c=P)).then_inc(small_in, 16)
            sp.dma_start(bv[:, :], b[KV0 + P:U0].partition_broadcast(P)).then_inc(small_in, 16)
            sp.dma_start(sink_b[:, :], sinks[0].partition_broadcast(P)).then_inc(small_in, 16)
            woa = w_o_attn[0].rearrange("(k p) n -> p k n", p=P)
            wop = w_o_pool[0].rearrange("(k p) n -> p k n", p=P)
            wo = w_out[0].rearrange("(k p) n -> p k n", p=P)

            def wait_step(name):
                i, before_ = turn(name)
                sp.wait_ge(bank_full[i], before_ + 1)

            for i, name in enumerate(MIX):
                s, j = i % SLOTS, int(name[-1])
                if i >= SLOTS:
                    wait_step(LAST[MIX[s]])
                got = mix_in[name]
                if name == "u0":
                    sp.dma_start(wmix[:, :, :], w_pool_mix[0].rearrange("g c d -> c g d")).then_inc(late_in, 16)
                    sp.dma_start(wrt[:, :, :], w_router[0].rearrange("(k p) e -> p k e", p=P)).then_inc(late_in, 16)
                    sp.dma_start(br_col[:, :], b_router[0].rearrange("(e i) -> e i", i=1)).then_inc(late_in, 16)
                if name[0] == "q":
                    sp.dma_start(slot(s, k=KD), w_in_v[:, :, j * 256:(j + 1) * 256]).then_inc(got, 16)
                elif name[:2] in ("u0", "u1"):
                    sp.dma_start(slot(s, k=KD), w_in_v[:, :, U0 + j * 256:U0 + (j + 1) * 256]).then_inc(got, 16)
                elif name[:2] in ("ga", "gp"):
                    c0 = (GA0 if name[1] == "a" else GP0) + j * 256
                    sp.dma_start(slot(s, k=KD), w_in_v[:, :, c0:c0 + 256]).then_inc(got, 16)
                elif name[:2] == "op":
                    sp.dma_start(slot(s, k=NG), wop[:, :, j * 512:(j + 1) * 512]).then_inc(got, 16)
                elif name[:2] == "oa":
                    sp.dma_start(slot(s, k=KD), woa[:, :, j * 256:(j + 1) * 256]).then_inc(got, 16)
                else:
                    sp.dma_start(slot(s, k=2), wo[:, 2 * j:2 * j + 2, :]).then_inc(got, 16)
            sp.wait_ge(scores_ready, 2)
            sp.dma_start(ln_g, ln1_g[0].partition_broadcast(P)).then_inc(ln1_in, 16)
            sp.dma_start(ln_b, ln1_b[0].partition_broadcast(P)).then_inc(ln1_in, 16)
            wait_step("o11")
            for i in range(3):
                rows_ = slice(i * NE, (i + 1) * NE)
                sp.dma_start(bias_raw[rows_, 0:2 * D], b_gu[0]).then_inc(bias_in, 16)
                sp.dma_start(bias_raw[rows_, 2 * D:], b_down[0]).then_inc(bias_in, 16)

            gu_v = w_gu[0].rearrange("e (k p) n -> e k p n", p=P)
            dn_v = w_down[0].rearrange("e (j k p) n -> e j p k n", k=2, p=P)

            def load_chunk(e, i, dst, got):
                if i < GU_CHUNKS:
                    sp.dma_start(dst, gu_v[e, i]).then_inc(got, 16)
                else:
                    sp.dma_start(dst.rearrange("p (k n) -> p k n", k=2), dn_v[e, i - GU_CHUNKS]).then_inc(got, 16)

            front, rear = range(len(annex)), range(len(annex), SLOTS)

            def load_first(q, e, chunks):
                for i in chunks:
                    sp.wait_ge(slot_free[i], q if i in front else 2 * q)
                    load_chunk(e, i, ring[:, i, :], slot_full[i])

            def load_second(q, e, chunks, fresh=False):
                for i in chunks:
                    if i in front:
                        if not fresh:
                            sp.wait_ge(annex_free[i], q)
                        load_chunk(e, i, annex[i], annex_full[i])
                    else:
                        sp.wait_ge(slot_free[i], 2 * q + 1)
                        load_chunk(e, i, ring[:, i, :], slot_full[i])

            early = [i for i in range(SLOTS) if not LAST[MIX[SLOTS + i]].startswith("h")]
            for i in early:
                wait_step(LAST[MIX[SLOTS + i]])
                load_chunk(0, i, ring[:, i, :], slot_full[i])
            for i in front[:-1]:
                if i == 0:
                    wait_step("o11")
                if i == NT + 1:
                    sp.wait_ge(merged, 4)
                load_second(0, 1, [i], fresh=True)
            for i in range(SLOTS):
                if i not in early:
                    wait_step(LAST[MIX[SLOTS + i]])
                    load_chunk(0, i, ring[:, i, :], slot_full[i])
            sp.wait_ge(normed, 2 * NT)
            load_second(0, 1, front[-1:], fresh=True)

            def load_on(q, e):
                load_first(q + 1, e + 2, front)
                load_second(q, e + 1, rear)
                load_second(q + 1, e + 3, front)
                load_first(q + 1, e + 2, rear)

            load_first(1, 2, front)
            load_second(0, 1, rear)
            load_second(1, 3, front)
            load_first(1, 2, rear)
            with sp.Fori(1, NE // 2 - 3) as q:
                load_on(q, 2 * q)
            last = NE // 2 - 1
            load_first(last - 1, NE - 4, front)
            load_second(last - 2, NE - 5, rear)
            load_second(last - 1, NE - 3, front[:4])
            load_first(last - 1, NE - 4, rear)
            load_second(last - 1, NE - 3, front[4:])
            load_first(last, NE - 2, front[:2])
            load_second(last - 1, NE - 3, rear)
            load_first(last, NE - 2, front[2:])
            load_second(last, NE - 1, front[:2])
            load_first(last, NE - 2, rear)
            load_second(last, NE - 1, front[2:])
            load_second(last, NE - 1, rear)
            sp.wait_ge(flag_ready, 1)
            over = sp.value_load(most_i[0:1, 0:1], min_val=0, max_val=SEQ)
            with sp.If(over > CAP):
                with sp.Fori(1, ROUNDS) as r:
                    with sp.Fori(0, NE // 2) as m:
                        load_first(r * (NE // 2) + m, 2 * m, range(SLOTS))
                        load_second(r * (NE // 2) + m, 2 * m + 1, range(SLOTS))
                sp.wait_ge(annex_free[-1], ROUNDS * NE // 2)
            sp.wait_ge(annex_free[-1], NE // 2)
            sp.dma_start(ln_g, ln2_g[0].partition_broadcast(P)).then_inc(ln2_in, 16)
            sp.dma_start(ln_b, ln2_b[0].partition_broadcast(P)).then_inc(ln2_in, 16)
            for t in range(NT):
                for i, cut in enumerate(halves):
                    if t == 0:
                        sp.wait_ge(pool_normed, i + 1)
                    else:
                        sp.wait_ge(normed, 2 * NT + i + 1)
                    sp.dma_start(out[0, t * P:(t + 1) * P, cut], xs[:, t, cut]).then_inc(out_done, 16)
            sp.wait_ge(out_done, 16 * NT * 2)

        @block.gpsimd
        def _(pool):
            pool.memset(ident[:, :], 0.0).then_inc(consts, 1)
            pool.memset(ones[:, :], 1.0).then_inc(consts, 1)
            pool.memset(sel3[:, :], 0.0).then_inc(consts, 1)
            pool.wait_ge(consts, 3)
            pool.affine_select(out=ident[:, :], in_=ident[:, :], compare_op=ALU.not_equal, fill=1.0, base=0,
                               pattern=[[-1, P]], channel_multiplier=1).then_inc(consts, 1)
            pool.memset(vs[0:CH, 0, :], 0.0).then_inc(consts, 1)
            pool.memset(ur[:, 0:NG * (PAD + SEQ)], 0.0).then_inc(consts, 1)
            pool.memset(oT[:, :], 0.0).then_inc(consts, 1)
            pool.memset(zeros[:, :], 0.0).then_inc(consts, 1)
            pool.affine_select(out=before[:, :], in_=ones[:, :], compare_op=ALU.is_gt, fill=0.0, base=0,
                               pattern=[[1, P]], channel_multiplier=-1).then_inc(consts, 1)
            pool.iota(slot_no[:, :, :], pattern=[[0, 2], [1, CAP]], base=0, channel_multiplier=0,
                      allow_small_or_imprecise_dtypes=True).then_inc(consts, 1)
            pool.iota(inv_n[:, :], pattern=[[1, PAD]], base=1, channel_multiplier=0,
                      allow_small_or_imprecise_dtypes=True).then_inc(consts, 1)
            for i in range(3):
                pool.affine_select(out=sel3[:, :], in_=sel3[:, :], compare_op=ALU.not_equal, fill=1.0,
                                   base=-i * NE, pattern=[[-1, NE]], channel_multiplier=1).then_inc(consts, 1)
                pool.wait_ge(consts, 12 + i)
            pool.wait_ge(bias_in, 6 * 16)
            step = 0
            for i in range(3):
                for j in range(i, 3):
                    rows_ = slice(j * NE, (j + 1) * NE)
                    pool.tensor_copy(bias3[rows_, :], bias_raw[rows_, :]).then_inc(pool_step, 1)
                step += 3 - i
                pool.wait_ge(pool_step, step)
                for j in range(i + 1, 3):
                    rows_ = slice(j * NE, (j + 1) * NE)
                    pool.tensor_tensor(bias_raw[rows_, :], bias_raw[rows_, :], bias3[rows_, :],
                                       ALU.subtract).then_inc(pool_step, 1)
                step += 2 - i
                pool.wait_ge(pool_step, step)
            pool.sem_inc(bias_split, 1)

            i, before_ = turn("logits1")
            pool.wait_ge(bank_full[i], before_ + 1)
            for h in range(2):
                pool.memset(ye[h], 0.0).then_inc(zeros_ready, 1)
            pool.memset(spreadT, 0.0).then_inc(zeros_ready, 1)
            pool.wait_ge(zeros_ready, 3)
            pool.sem_inc(ye_ready, 1)
            pool.sem_inc(ye2_ready, 1)
            pool.sem_inc(spreadT_ready, 1)

            pool.wait_ge(ln2_in, 2 * 16)
            for i, cut in enumerate(halves):
                pool.wait_ge(act_normed, i + 1)
                pool.tensor_tensor(xs[:, 0, cut], xs[:, 0, cut], ln_g[:, cut], ALU.mult).then_inc(scaled, 1)
                pool.wait_ge(scaled, i + 1)
                pool.tensor_tensor(xs[:, 0, cut], xs[:, 0, cut], ln_b[:, cut], ALU.add).then_inc(pool_normed, 1)
        CONSTS = 14

        @block.scalar
        def _(act):
            def full(name):
                i, before_ = turn(name)
                act.wait_ge(bank_full[i], before_ + 1)
                return bank[i]

            def free(name):
                return bank_free[turn(name)[0]]

            def turn_x(c):
                t, g = c // 2, c % 2
                ps = full(f"x{c}")
                act.activation(feat[:, 4 * g:4 * g + 4, t * P:(t + 1) * P],
                               ps[:, :].rearrange("p (k s) -> p k s", k=4), ACT.Copy).then_inc(free(f"x{c}"), 1)

            turn_x(0)
            turn_x(2)
            i, before_ = turn("v")
            act.wait_ge(bank_free[i], before_ + 1)
            act.dma_start(vs[CH:P, 0, :], vs[0:CH, 1, :]).then_inc(v_moved, 16)
            act.dma_start(vs[0:CH, 2, :], vs[CH:P, 1, :]).then_inc(v_moved, 16)
            act.dma_start(vs[CH:P, 2, :], vs[0:CH, 3, :]).then_inc(v_moved, 16)
            i, before_ = turn("k")
            act.wait_ge(bank_free[i], before_ + 1)
            for g in range(NKV):
                act.dma_start(kT[g * HD:(g + 1) * HD, 1, :],
                              kT[(1 - g) * HD:(2 - g) * HD, 0, :]).then_inc(k_moved, 16)
            for j in range(4):
                ps = full(f"q{j}")
                if j == 0:
                    act.wait_ge(bank_free[turn("rows")[0]], turn("rows")[1] + 1)
                for i in range(2):
                    m = 2 * j + i
                    ins = act.activation(qT[:, m, :], ps[:, i * SEQ:(i + 1) * SEQ], ACT.Identity,
                                         bias=cols[:, m:m + 1])
                ins.then_inc(free(f"q{j}"), 1)

            for t in range(NT):
                act.wait_ge(shifted, t + 1)
                act.activation(probs[:, t, :], probs[:, t, :], ACT.Exp).then_inc(act_step, 1)
                act.activation(sden[:, t, :], sden[:, t, :], ACT.Exp).then_inc(exps_ready, 1)

            def sigmoid(a, j):
                name = f"g{'ap'[a]}{j}"
                ps = full(name)
                for i in range(2):
                    m = 2 * j + i
                    c = 13 + a * KD + m
                    ins = act.activation(gates[:, a, m, :], ps[:, i * SEQ:(i + 1) * SEQ], ACT.Sigmoid,
                                         bias=cols[:, c:c + 1])
                ins.then_inc(free(name), 1)

            def turn_probs(t):
                for c in (0, 2):
                    name = f"pt{t}{c}"
                    ps = full(name)
                    act.activation(probsT[t][:, 4 * c:4 * c + 4, :],
                                   ps[:, :].rearrange("p (h q) -> p h q", h=4), ACT.Copy).then_inc(free(name), 1)

            for j in range(4):
                sigmoid(0, j)
            turn_probs(0)
            sigmoid(1, 0)
            sigmoid(1, 1)
            turn_probs(1)
            sigmoid(1, 2)
            sigmoid(1, 3)

            def root(i):
                act.wait_ge(var_ready, i + 1)
                act.activation(rstd[:, i % NT, :], rstd[:, i % NT, :], ACT.Sqrt).then_inc(std_ready, 1)

            def take_normed(t):
                for g in range(2):
                    ps = full(f"t{2 * t + g}")
                    act.activation(feat[:, 4 * g:4 * g + 4, t * P:(t + 1) * P],
                                   ps[:, :].rearrange("p (k s) -> p k s", k=4),
                                   ACT.Copy).then_inc(free(f"t{2 * t + g}"), 1)

            def take_logits(t):
                act.activation(logitT[:, t, :], full(f"logits{t}")[0:NE, 0:P], ACT.Identity,
                               bias=br_col[:, :]).then_inc(logitT_ready, 1)

            root(0)
            take_normed(0)
            root(1)
            act.wait_ge(late_in, 3 * 16)
            take_logits(0)
            take_normed(1)
            take_logits(1)
            act.wait_ge(top_shift, 1)
            act.activation(tex[:, :, :], tex[:, :, :], ACT.Exp).then_inc(top_exp, 1)

            def take_gathered(q):
                for i, ps in enumerate((turn_ps, down_ps)):
                    act.wait_ge(gathered, 2 * q + i + 1)
                    ins = act.activation(xg[:, 4 * i:4 * i + 4, :, :],
                                         ps[:, :].rearrange("p (k i j) -> p k i j", k=4, i=2), ACT.Copy)
                ins.then_inc(xg_ready, 1)

            def take_sigmoid(n):
                act.wait_ge(gate_clamped, n + 1)
                act.activation(sig, gate_c, ACT.Sigmoid, scale=SW_ALPHA).then_inc(sig_ready, 1)

            def take_rows(n, i):
                act.wait_ge(down_done, n + 1)
                part = slice(CAP * i, CAP * i + CAP)
                act.activation(ye[0][part, :], down_ps[part, :], ACT.Copy).then_inc(ye_ready, 1)

            def pair(q, more=True):
                take_sigmoid(2 * q)
                take_rows(2 * q, 0)
                take_sigmoid(2 * q + 1)
                if more:
                    take_gathered(q + 1)
                act.wait_ge(spread_turned, q + 1)
                act.activation(spreadT, gate_ps[:, :].rearrange("p (t h q) -> p t h q", t=NT, h=2),
                               ACT.Copy).then_inc(spreadT_ready, 1)
                take_rows(2 * q + 1, 1)

            act.wait_ge(bias_split, 1)
            take_gathered(0)
            pair(0)
            with act.Fori(1, NE // 2 - 1) as q:
                pair(q)
            pair(NE // 2 - 1, more=False)
            act.wait_ge(flag_ready, 1)
            over = act.value_load(most_i[0:1, 0:1], min_val=0, max_val=SEQ)
            with act.If(over > CAP):
                take_gathered(NE // 2)
                with act.Fori(NE // 2, ROUNDS * NE // 2 - 1) as q:
                    pair(q)
                pair(ROUNDS * NE // 2 - 1, more=False)
            root(NT)
            act.wait_ge(scale_ready, 1)
            for cut in halves:
                act.activation(xs[:, 0, cut], xs[:, 0, cut], ACT.Identity, bias=shift[:, :],
                               scale=rstd[:, 0, :]).then_inc(act_normed, 1)
            root(NT + 1)

        @block.tensor
        def _(pe):
            pe.wait_ge(consts, 4)

            def take(name):
                i, before_ = turn(name)
                if before_:
                    pe.wait_ge(bank_free[i], before_)
                return bank[i]

            def full(name):
                return bank_full[turn(name)[0]]

            for c in range(4):
                t, g = c // 2, c % 2
                pe.wait_ge(x_in[c], 16)
                ps = take(f"x{c}")
                for k in range(4):
                    mm = pe.transpose(ps[:, k * P:(k + 1) * P], xs[:, t, (4 * g + k) * P:(4 * g + k + 1) * P],
                                      ident[:, :])
                mm.then_inc(full(f"x{c}"), 1)
            xT = feat[:, :, :]
            ps = take("k")
            for c in range(4):
                pe.wait_ge(bank_free[turn(f"x{c}")[0]], turn(f"x{c}")[1] + 1)
            for k in range(KD):
                if k % 4 == 0:
                    pe.wait_ge(mix_in[f"kv{k // 4}"], 16)
                mm = pe.matmul(ps[:, 0:SEQ], kv_w[:, k, 0:P], xT[:, k, :], start=(k == 0), stop=(k == KD - 1))
            mm.then_inc(full("k"), 1)
            ps = take("v")
            for t in range(NT):
                for k in range(KD):
                    mm = pe.matmul(ps[:, t * P:(t + 1) * P], xT[:, k, t * P:(t + 1) * P], kv_w[:, k, P:2 * P],
                                   start=(k == 0), stop=(k == KD - 1))
            mm.then_inc(full("v"), 1)
            ps = take("rows")
            pe.wait_ge(small_in, 5 * 16)
            pe.transpose(ps[:, 0:33], rows[:, :], ident[0:33, 0:33]).then_inc(full("rows"), 1)

            def project(name, weight, rhs, ks):
                ps = take(name)
                for i in range(2):
                    for k in range(ks):
                        mm = pe.matmul(ps[:, i * SEQ:(i + 1) * SEQ], weight(k, i), rhs(k),
                                       start=(k == 0), stop=(k == ks - 1))
                mm.then_inc(full(name), 1)

            def from_x(name):
                s = MIX.index(name) % SLOTS
                pe.wait_ge(mix_in[name], 16)
                project(name, lambda k, i: slot(s, k=KD)[:, k, i * P:(i + 1) * P], lambda k: xT[:, k, :], KD)

            def score(t):
                if t == 0:
                    pe.wait_ge(mask_set, 1)
                    pe.wait_ge(k_moved, 2 * 16)
                    for name in ("k", "q0", "q1", "q2", "q3"):
                        pe.wait_ge(bank_free[turn(name)[0]], turn(name)[1] + 1)
                else:
                    pe.wait_ge(scores_read, 1)
                for m in range(KD):
                    for i in range(2):
                        rows_ = slice(i * HD, (i + 1) * HD)
                        swap = i ^ (m // (KD // 2))
                        for half in range(2):
                            c = 2 * t + half
                            lo = CH if c == 0 else 0
                            mm = pe.matmul(scores[half * CH:(half + 1) * CH, i * KD + m, lo:P],
                                           qT[rows_, m, c * CH:(c + 1) * CH],
                                           kT[rows_, swap, (c - 1) * CH + lo:(c + 1) * CH],
                                           start=True, stop=True)
                mm.then_inc(scores_ready, 1)

            def turn_probs(t):
                pe.wait_ge(probs_ready, t + 1)
                for c in range(4):
                    name = f"pt{t}{c}"
                    ps = take(name)
                    for h in range(4):
                        mm = pe.transpose(ps[:, h * P:(h + 1) * P],
                                          probs[:, t, (4 * c + h) * P:(4 * c + h + 1) * P], ident[:, :])
                    mm.then_inc(full(name), 1)

            def attend(t):
                pe.wait_ge(v_moved, 3 * 16)
                for c in range(4):
                    pe.wait_ge(bank_free[turn(f"pt{t}{c}")[0]], turn(f"pt{t}{c}")[1] + 1)
                for half in range(2):
                    c = 2 * t + half
                    name = f"o{t}{half}"
                    ps = take(name)
                    for g in range(NKV):
                        for i in range(2):
                            mm = pe.matmul(ps[i * HD:(i + 1) * HD, g * SEQ:(g + 1) * SEQ],
                                           vs[:, c, g * HD:(g + 1) * HD],
                                           probsT[t][:, i * KD + g * HG:i * KD + (g + 1) * HG,
                                                     half * CH:(half + 1) * CH],
                                           start=True, stop=True)
                    mm.then_inc(full(name), 1)

            for j in range(4):
                from_x(f"q{j}")
            from_x("u0")
            score(0)
            from_x("u1")
            score(1)
            for j in range(4):
                from_x(f"ga{j}")
            pe.wait_ge(late_in, 3 * 16)
            pe.wait_ge(pooled, NG)
            for j in range(2):
                ps = take(f"mix{j}")
                for i in range(2):
                    g = 2 * j + i
                    mm = pe.matmul(ps[:, i * SEQ:(i + 1) * SEQ], wmix[:, g, :], rT[:, g, :], start=True, stop=True)
                mm.then_inc(full(f"mix{j}"), 1)
            for t in range(NT):
                turn_probs(t)
                from_x(f"gp{2 * t}")
                attend(t)
                from_x(f"gp{2 * t + 1}")
            for j in range(2):
                pe.wait_ge(bank_free[turn(f"mix{j}")[0]], turn(f"mix{j}")[1] + 1)
            for j in range(4):
                s = MIX.index(f"op{j // 2}") % SLOTS
                pe.wait_ge(mix_in[f"op{j // 2}"], 16)
                project(f"yp{j}",
                        lambda k, i: slot(s, k=NG)[:, k, (j % 2) * 256 + i * P:(j % 2) * 256 + (i + 1) * P],
                        lambda k: uT[:, k, PAD:PAD + SEQ], NG)
            for t in range(NT):
                for half in range(2):
                    pe.wait_ge(bank_free[turn(f"o{t}{half}")[0]], turn(f"o{t}{half}")[1] + 1)
            for j in range(4):
                s = MIX.index(f"oa{j}") % SLOTS
                pe.wait_ge(mix_in[f"oa{j}"], 16)
                project(f"ya{j}", lambda k, i: slot(s, k=KD)[:, k, i * P:(i + 1) * P],
                        lambda k: o_heads[:, k, :], KD)
            for t in range(NT):
                for half in range(2):
                    name = f"h{t}{half}"
                    ps = take(name)
                    for k in range(KD):
                        pe.wait_ge(merged, k // 2 + 1)
                        pe.wait_ge(mix_in[f"wo{k // 2}"], 16)
                        s = MIX.index(f"wo{k // 2}") % SLOTS
                        mm = pe.matmul(ps[:, :], feat[:, k, t * P:(t + 1) * P],
                                       slot(s, k=2)[:, k % 2, half * 512:(half + 1) * 512],
                                       start=(k == 0), stop=(k == KD - 1))
                    mm.then_inc(full(name), 1)

            def turn_normed(t):
                for c in (2 * t, 2 * t + 1):
                    pe.wait_ge(normed, c + 1)
                    ps = take(f"t{c}")
                    for k in range(4):
                        kk = 4 * (c % 2) + k
                        mm = pe.transpose(ps[:, k * P:(k + 1) * P], xs[:, t, kk * P:(kk + 1) * P], ident[:, :])
                    mm.then_inc(full(f"t{c}"), 1)

            def logits(t):
                ps = take(f"logits{t}")
                for c in (2 * t, 2 * t + 1):
                    pe.wait_ge(bank_free[turn(f"t{c}")[0]], turn(f"t{c}")[1] + 1)
                for k in range(KD):
                    mm = pe.matmul(ps[0:NE, 0:P], wrt[:, k, :], feat[:, k, t * P:(t + 1) * P],
                                   start=(k == 0), stop=(k == KD - 1))
                mm.then_inc(full(f"logits{t}"), 1)

            def turn_logits(t):
                pe.wait_ge(logitT_ready, t + 1)
                pe.transpose(logit_ps[t], logitT[:, t, :], ident[0:NE, 0:NE]).then_inc(logit_turned, 1)

            turn_normed(0)
            for i in range(4):
                pe.matmul(wide[:, i, :], zeros[:, 0:P], zeros[:, :], start=True, stop=False, skip_group_check=True)
            logits(0)
            for i in range(3):
                pe.matmul(wide[:, i, :], zeros[:, 0:P], zeros[:, :], start=False, stop=False, skip_group_check=True)
            turn_logits(0)
            turn_normed(1)
            pe.wait_ge(chosen_ready, 1)
            pe.matmul(rank0_ps, before[:, :], chosen[:, 0, :], start=True, stop=True).then_inc(rank0_done, 1)
            logits(1)
            for name in ("t2", "t3"):
                pe.wait_ge(bank_free[turn(name)[0]], turn(name)[1] + 1)
            for ps in (down_ps, turn_ps):
                pe.matmul(ps[:, :], zeros[:, 0:P], zeros[:, :], start=True, stop=False, skip_group_check=True)
            turn_logits(1)
            pe.wait_ge(pick_first, 1)

            def gather_first(t, ks):
                for k in ks:
                    mm = pe.matmul((turn_ps, down_ps)[k // 4][:, (k % 4) * P:(k % 4 + 1) * P],
                                   xs[:, t, k * P:(k + 1) * P], pick[:, t, :, :],
                                   start=False, stop=(t == NT - 1), skip_group_check=True)
                    if t == NT - 1 and k % 4 == 3:
                        mm.then_inc(gathered, 1)

            gather_first(0, range(KD // 2))
            pe.wait_ge(chosen_ready, 2)
            ps = take("rank1")
            pe.matmul(ps[:, 0:NE], ones[:, :], chosen[:, 0, :], start=True, stop=False)
            pe.matmul(ps[:, 0:NE], before[:, :], chosen[:, 1, :], start=False, stop=True)
            pe.matmul(ps[:, NE:2 * NE], ones[:, :], chosen[:, 0, :], start=True, stop=False)
            pe.matmul(ps[:, NE:2 * NE], ones[:, :], chosen[:, 1, :], start=False,
                      stop=True).then_inc(full("rank1"), 1)
            gather_first(0, range(KD // 2, KD))
            pe.wait_ge(pick_ready, 1)
            gather_first(1, range(KD))

            def gather(q):
                pe.wait_ge(pick_ready, q + 1)
                for k in range(KD):
                    for t in range(NT):
                        mm = pe.matmul((turn_ps, down_ps)[k // 4][:, (k % 4) * P:(k % 4 + 1) * P],
                                       xs[:, t, k * P:(k + 1) * P], pick[:, t, :, :],
                                       start=(t == 0), stop=(t == NT - 1))
                    if k % 4 == 3:
                        mm.then_inc(gathered, 1)

            def combine(t, half, stop):
                return pe.matmul(wide[:, 2 * t + half, :], spreadT[:, t, half, :], ye[half],
                                 start=False, stop=stop, skip_group_check=True)

            def gate_up(n, i, spot):
                pieces = [(ps, half, (2 * c + half) * 512)
                          for c, ps in enumerate((gate_ps, up_ps)) for half in range(2)]

                def bias(piece, start):
                    ps, half, col = piece
                    return pe.matmul(ps[half * CAP:(half + 1) * CAP, :], one_e[:, i, :], bias3[:, col:col + 512],
                                     start=start, stop=not start)

                for piece in pieces[:3]:
                    bias(piece, True)
                for k in range(GU_CHUNKS):
                    w, got, count, freed = spot(k)
                    pe.wait_ge(got, count)
                    for j, (ps, half, col) in enumerate(pieces):
                        last = k == GU_CHUNKS - 1
                        mm = pe.matmul(ps[half * CAP:(half + 1) * CAP, :], xg[:, k, i, :], w[:, col:col + 512],
                                       start=(k == 0 and j == 3), stop=(last and j < 3))
                        if last and j == 1:
                            mm.then_inc(gate_done, 1)
                    mm.then_inc(freed, 1)
                bias(pieces[3], False).then_inc(up_done, 1)

            def turn_act(n):
                pe.wait_ge(act_ready, n + 1)
                for f in range(4):
                    mm = pe.transpose(turn_ps[:, f * P:(f + 1) * P], up_c[:, f * P:(f + 1) * P], ident[:, :])
                mm.then_inc(act_turned, 1)

            def down(n, i, spot):
                pe.wait_ge(actT_ready, n + 1)
                pe.wait_ge(ye_ready, n + 1)
                pe.wait_ge(ye2_ready, n + 1)

                def bias(half, start):
                    part = CAP * (half ^ i)
                    return pe.matmul(down_ps[part:part + CAP, :], one_e[:, i, :],
                                     bias3[:, 2 * D + half * 512:2 * D + (half + 1) * 512],
                                     start=start, stop=not start)

                bias(0, True)
                for k in range(KD):
                    w, got, count, freed = spot(GU_CHUNKS + k // 2)
                    if k % 2 == 0:
                        pe.wait_ge(got, count)
                    for half in range(2):
                        part = CAP * (half ^ i)
                        mm = pe.matmul(down_ps[part:part + CAP, :], actT[:, k % 4, k // 4, :],
                                       w[:, (k % 2) * D + half * 512:(k % 2) * D + (half + 1) * 512],
                                       start=(k == 0 and half == 1), stop=(k == KD - 1 and half == 0))
                    if k % 2:
                        mm.then_inc(freed, 1)
                bias(1, False).then_inc(down_done, 1)

            def first_spot(q):
                return lambda c: (ring[:, c, :], slot_full[c], 16 * (q + 1 if c < len(annex) else 2 * q + 1),
                                  slot_free[c])

            def second_spot(q):
                return lambda c: ((annex[c], annex_full[c], 16 * (q + 1), annex_free[c]) if c < len(annex) else
                                  (ring[:, c, :], slot_full[c], 16 * (2 * q + 2), slot_free[c]))

            def pair(q, more=True):
                n = 2 * q
                first, second = first_spot(q), second_spot(q)
                pe.wait_ge(xg_ready, q + 1)
                pe.wait_ge(spreadT_ready, q + 1)
                pe.wait_ge(one_ready, q + 1)
                gate_up(n, 0, first)
                pe.wait_ge(ye_ready, n + 1)
                pe.wait_ge(ye2_ready, n + 1)
                for t in range(NT):
                    for half in range(2):
                        combine(t, half, False)
                turn_act(n)
                down(n, 0, first)
                gate_up(n + 1, 1, second)
                if more:
                    pe.wait_ge(ye_ready, n + 2)
                    pe.wait_ge(ye2_ready, n + 2)
                    gather(q + 1)
                    pe.wait_ge(xg_ready, q + 2)
                turn_act(n + 1)
                pe.wait_ge(spread_ready, q + 1)
                for t in range(NT):
                    for h in range(2):
                        mm = pe.transpose(gate_ps[:, (2 * t + h) * P:(2 * t + h + 1) * P],
                                          spread[:, t, h:h + 2, :].rearrange("p i j -> p (i j)"), ident[:, :])
                mm.then_inc(spread_turned, 1)
                down(n + 1, 1, second)

            pair(0)
            with pe.Fori(1, NE // 2 - 1) as q:
                pair(q)
            pair(NE // 2 - 1, more=False)
            pe.wait_ge(flag_ready, 1)
            over = pe.value_load(most_i[0:1, 0:1], min_val=0, max_val=SEQ)
            with pe.If(over > CAP):
                pe.wait_ge(ye_ready, NE + 1)
                pe.wait_ge(ye2_ready, NE + 1)
                gather(NE // 2)
                with pe.Fori(NE // 2, ROUNDS * NE // 2 - 1) as q:
                    pair(q)
                pair(ROUNDS * NE // 2 - 1, more=False)
                pe.wait_ge(ye_ready, ROUNDS * NE + 1)
                pe.wait_ge(ye2_ready, ROUNDS * NE + 1)
            pe.wait_ge(ye_ready, NE + 1)
            pe.wait_ge(ye2_ready, NE + 1)
            for t in range(NT):
                for half in range(2):
                    combine(t, half, True).then_inc(moe_done, 1)

        @block.vector
        def _(dve):
            done = [0]

            def then(ins):
                done[0] += 1
                ins.then_inc(dve_step, 1)
                dve.wait_ge(dve_step, done[0])

            def full(name):
                i, before_ = turn(name)
                dve.wait_ge(bank_full[i], before_ + 1)
                return bank[i]

            def free(name):
                return bank_free[turn(name)[0]]

            dve.memset(scores[0:CH, :, 0:CH], NEG).then_inc(mask_set, 1)
            for c in (1, 3):
                t, g = c // 2, c % 2
                ps = full(f"x{c}")
                dve.tensor_copy(feat[:, 4 * g:4 * g + 4, t * P:(t + 1) * P],
                                ps[:, :].rearrange("p (k s) -> p k s", k=4)).then_inc(free(f"x{c}"), 1)
            dve.wait_ge(consts, CONSTS)
            then(dve.reciprocal(inv_n[:, :], inv_n[:, :]))
            dve.wait_ge(small_in, 5 * 16)
            ps = full("v")
            dve.tensor_tensor(vs[:, 1::2, :], ps[:, 0:2 * P].rearrange("p (c n) -> p c n", c=2),
                              bv[:, :].unsqueeze(1).to_broadcast([P, 2, P]), ALU.add).then_inc(free("v"), 1)
            ps = full("rows")
            dve.tensor_copy(cols[:, :], ps[:, 0:33]).then_inc(free("rows"), 1)
            dve.wait_ge(free("rows"), turn("rows")[1] + 1)
            ps = full("k")
            dve.tensor_scalar(kT[:, 0, :], ps[:, 0:SEQ], cols[:, 8:9], None, ALU.add).then_inc(free("k"), 1)

            def softmax_shift(t):
                dve.wait_ge(scores_ready, t + 1)
                then(dve.tensor_reduce(smax[:, t, :], scores, AX.X, ALU.max))
                by_head = [a[:, t, :].rearrange("p (i m) -> p i m", i=2) for a in (smax, sden)]
                sinks_ = sink_b[:, :].rearrange("p (m i) -> p i m", i=2)
                then(dve.scalar_tensor_tensor(out=by_head[0], in0=by_head[0], scalar=HD ** -0.5,
                                              in1=sinks_, op0=ALU.mult, op1=ALU.max))
                dve.tensor_tensor(by_head[1], sinks_, by_head[0], ALU.subtract).then_inc(dve_step, 1)
                done[0] += 1
                then(dve.scalar_tensor_tensor(out=probs[:, t, :].rearrange("p (h k) -> p h k", h=NH), in0=scores,
                                              scalar=HD ** -0.5,
                                              in1=smax[:, t, :].unsqueeze(2).to_broadcast([P, NH, P]),
                                              op0=ALU.mult, op1=ALU.subtract))
                dve.sem_inc(scores_read, 1)
                dve.sem_inc(shifted, 1)

            def softmax_norm(t):
                p3 = probs[:, t, :].rearrange("p (h k) -> p h k", h=NH)
                dve.wait_ge(act_step, t + 1)
                dve.wait_ge(exps_ready, t + 1)
                then(dve.tensor_reduce(ssum[:, t, :], p3, AX.X, ALU.add))
                then(dve.tensor_tensor(sden[:, t, :], sden[:, t, :], ssum[:, t, :], ALU.add))
                then(dve.reciprocal(sden[:, t, :], sden[:, t, :]))
                dve.tensor_tensor(p3, p3, sden[:, t, :].unsqueeze(2).to_broadcast([P, NH, P]),
                                  ALU.mult).then_inc(probs_ready, 1)

            softmax_shift(0)
            for j in range(2):
                ps = full(f"u{j}")
                for i in range(2):
                    g = 2 * j + i
                    ins = dve.tensor_scalar(uT[:, g, PAD:], ps[:, i * SEQ:(i + 1) * SEQ], cols[:, 9 + g:10 + g],
                                            None, ALU.add)
                ins.then_inc(free(f"u{j}"), 1)
            dve.wait_ge(free("u1"), turn("u1")[1] + 1)
            softmax_shift(1)
            softmax_norm(0)
            src = uT
            for step in range(NG):
                w = 1 << step
                dst = sums[step % 2]
                then(dve.tensor_tensor(dst[:, step:, PAD:], src[:, step:, PAD:], src[:, step:, PAD - w:PAD + SEQ - w],
                                       ALU.add))
                src = dst
            for g in range(NG):
                w = 2 << g
                s = sums[g % 2]
                then(dve.scalar_tensor_tensor(out=rT[:, g, :], in0=s[:, g, PAD:], scalar=1.0 / w,
                                              in1=uT[:, g, PAD:], op0=ALU.mult, op1=ALU.subtract))
                then(dve.tensor_tensor(s[:, g, PAD:PAD + w - 1], s[:, g, PAD:PAD + w - 1], inv_n[:, 0:w - 1],
                                       ALU.mult))
                dve.tensor_tensor(rT[:, g, 0:w - 1], s[:, g, PAD:PAD + w - 1], uT[:, g, PAD:PAD + w - 1],
                                  ALU.subtract).then_inc(pooled, 1)
            dve.wait_ge(pooled, NG)
            softmax_norm(1)
            for j in range(2):
                ps = full(f"mix{j}")
                for i in range(2):
                    g = 2 * j + i
                    ins = dve.tensor_scalar(uT[:, g, PAD:], ps[:, i * SEQ:(i + 1) * SEQ], cols[:, 29 + g:30 + g],
                                            None, ALU.mult)
                ins.then_inc(free(f"mix{j}"), 1)

            def turn_probs(t):
                for c in (1, 3):
                    name = f"pt{t}{c}"
                    ps = full(name)
                    dve.tensor_copy(probsT[t][:, 4 * c:4 * c + 4, :],
                                    ps[:, :].rearrange("p (h q) -> p h q", h=4)).then_inc(free(name), 1)

            def take_attended(t):
                for half in range(2):
                    c = 2 * t + half
                    name = f"o{t}{half}"
                    ps = full(name)
                    dve.tensor_copy(o_heads[:, :, c * CH:(c + 1) * CH],
                                    ps[:, :].rearrange("p (m q) -> p m q", m=KD)).then_inc(free(name), 1)

            for t in range(NT):
                turn_probs(t)
                take_attended(t)

            for a, branch in ((1, "yp"), (0, "ya")):
                for j in range(4):
                    name = f"{branch}{j}"
                    ps = full(name)
                    gname = f"g{'ap'[a]}{j}"
                    dve.wait_ge(free(gname), turn(gname)[1] + 1)
                    g = gates[:, a, 2 * j:2 * j + 2, :]
                    dve.tensor_tensor(g, g, ps[:, :].rearrange("p (i s) -> p i s", i=2),
                                      ALU.mult).then_inc(free(name), 1)
                    if a == 0:
                        dve.wait_ge(free(name), turn(name)[1] + 1)
                        dve.tensor_tensor(feat[:, 2 * j:2 * j + 2, :], g, gates[:, 1, 2 * j:2 * j + 2, :],
                                          ALU.add).then_inc(merged, 1)

            def add_residual(t, half, part):
                z = xs[:, t, halves[half]]
                then(dve.scalar_tensor_tensor(out=z, in0=z, scalar=ALPHA, in1=part, op0=ALU.mult, op1=ALU.add))

            def moments(t, half):
                then(dve.bn_stats(stats[:, t, half, :], xs[:, t, halves[half]]))

            def variance(t):
                then(dve.bn_aggr(mv[:, t, :], stats[:, t, :, :]))
                dve.tensor_scalar(rstd[:, t, :], mv[:, t, 1:2], EPS, None, ALU.add).then_inc(var_ready, 1)

            def center(t, cut):
                then(dve.scalar_tensor_tensor(out=xs[:, t, cut], in0=xs[:, t, cut], scalar=mv[:, t, 0:1],
                                              in1=ln_g[:, cut], op0=ALU.subtract, op1=ALU.mult))

            def invert(i):
                dve.wait_ge(std_ready, i + 1)
                then(dve.reciprocal(rstd[:, i % NT, :], rstd[:, i % NT, :]))

            def scale(t, cut):
                dve.scalar_tensor_tensor(out=xs[:, t, cut], in0=xs[:, t, cut], scalar=rstd[:, t, :], in1=ln_b[:, cut],
                                         op0=ALU.mult, op1=ALU.add).then_inc(normed, 1)

            for t in range(NT):
                for half in range(2):
                    add_residual(t, half, full(f"h{t}{half}")[:, :])
                    dve.sem_inc(free(f"h{t}{half}"), 1)
                    moments(t, half)
                variance(t)
                dve.wait_ge(ln1_in, 2 * 16)
                center(t, slice(0, D))
                invert(t)
                for half in halves:
                    scale(t, half)

            dve.wait_ge(late_in, 3 * 16)
            expert_no = slot_no[:, 0, 0:NE]

            def choose(t):
                dve.wait_ge(logit_turned, t + 1)
                then(dve.max(top[:, t, :], logit_ps[t]))
                then(dve.max_index(topi[:, t, :], top[:, t, :], logit_ps[t]))
                dve.sem_inc(free(f"logits{t}"), 1)
                then(dve.tensor_copy(topf[:, t, :], topi[:, t, 0:TOPK]))
                then(dve.tensor_tensor(hit[:, t, :, :], expert_no.unsqueeze(1).to_broadcast([P, TOPK, NE]),
                                       topf[:, t, :].unsqueeze(2).to_broadcast([P, TOPK, NE]), ALU.is_equal))
                then(dve.tensor_reduce(rank1[:, t, :], hit[:, t, :, :].rearrange("p s e -> p e s"), AX.X, ALU.add))
                dve.tensor_copy(chosen[:, t, :], rank1[:, t, :]).then_inc(chosen_ready, 1)

            def pick_tile(q, t):
                for i in range(2):
                    ins = dve.tensor_scalar(pick[:, t, i, :], slot_no[:, 0, :],
                                            rank_n[:, t, bass.ds(2 * q + i, 1)], None, ALU.is_equal)
                return ins

            def place(t, ranks):
                then(dve.scalar_tensor_tensor(out=rank1[:, t, :], in0=ranks, scalar=1.0, in1=rank1[:, t, :],
                                              op0=ALU.add, op1=ALU.mult))
                then(dve.tensor_scalar(rank_n[:, t, 0:NE], rank1[:, t, :], 1.0, None, ALU.subtract))

            def choose_one(e):
                for i in range(2):
                    ins = dve.tensor_copy(one_e[:, i, :], sel3[:, bass.ds(e + i, 1)].to_broadcast([3 * NE, CAP]))
                ins.then_inc(one_ready, 1)

            choose(0)
            dve.wait_ge(rank0_done, 1)
            place(0, rank0_ps)
            pick_tile(0, 0).then_inc(pick_first, 1)
            choose_one(0)
            choose(1)
            ps = full("rank1")
            place(1, ps[:, 0:NE])
            dve.tensor_reduce(most[:, :], ps[:, NE:2 * NE], AX.X, ALU.max).then_inc(dve_step, 1)
            done[0] += 1
            pick_tile(0, 1).then_inc(pick_ready, 1)
            dve.tensor_tensor(tex[:, :, :], top[:, :, 0:TOPK], top[:, :, 0:1].to_broadcast([P, NT, TOPK]),
                              ALU.subtract).then_inc(top_shift, 1)

            def pick_pair(q):
                for t in range(NT):
                    ins = pick_tile(q, t)
                ins.then_inc(pick_ready, 1)

            dve.wait_ge(dve_step, done[0])
            dve.tensor_copy(most_i[:, :], most[:, :]).then_inc(flag_ready, 1)
            then(dve.memset(rank_n[:, :, ROUNDS * NE:], -1.0))
            for r in range(1, ROUNDS):
                then(dve.tensor_scalar(rank_n[:, :, r * NE:(r + 1) * NE], rank1[:, :, :], 1.0 + r * CAP, None,
                                       ALU.subtract))
            dve.wait_ge(top_exp, 1)
            then(dve.tensor_reduce(tsum[:, :], tex[:, :, :], AX.X, ALU.add))
            then(dve.reciprocal(tsum[:, :], tsum[:, :]))
            then(dve.tensor_tensor(tex[:, :, :], tex[:, :, :], tsum[:, :].unsqueeze(2).to_broadcast([P, NT, TOPK]),
                                   ALU.mult))
            then(dve.tensor_tensor(hitg.rearrange("p t s e -> p (t s) e"), hit.rearrange("p t s e -> p (t s) e"),
                                   tex[:, :, :].rearrange("p t s -> p (t s)").unsqueeze(2)
                                   .to_broadcast([P, NT * TOPK, NE]), ALU.mult))
            then(dve.tensor_reduce(gate1[:, :, :], hitg.rearrange("p t s e -> p t e s"), AX.X, ALU.add))
            for r in range(ROUNDS):
                then(dve.tensor_copy(gate_n[:, :, r * NE:(r + 1) * NE], gate1[:, :, :]))

            def swiglu(n):
                dve.wait_ge(gate_done, n + 1)
                dve.tensor_scalar(gate_c, gate_ps[:, :], SW_LIMIT, None, ALU.min).then_inc(gate_clamped, 1)
                dve.wait_ge(up_done, n + 1)
                dve.tensor_scalar(up_c, up_ps[:, :], -SW_LIMIT, SW_LIMIT, ALU.max, ALU.min).then_inc(up_clamped, 1)
                dve.wait_ge(gate_clamped, n + 1)
                dve.wait_ge(up_clamped, n + 1)
                dve.scalar_tensor_tensor(out=up_c, in0=up_c, scalar=1.0, in1=gate_c, op0=ALU.add,
                                         op1=ALU.mult).then_inc(gated, 1)
                dve.wait_ge(gated, n + 1)
                dve.wait_ge(sig_ready, n + 1)
                dve.tensor_tensor(up_c, up_c, sig, ALU.mult).then_inc(act_ready, 1)
                dve.wait_ge(act_turned, n + 1)
                dve.tensor_copy(actT, turn_ps[:, :].rearrange("p (f h j) -> p f h j", f=4, h=2)).then_inc(actT_ready, 1)

            def pair(q, e, starting=False):
                if not starting:
                    dve.wait_ge(down_done, 2 * q)
                    choose_one(e)
                dve.wait_ge(gathered, 2 * q + 2)
                pick_pair(q + 1)
                if not starting:
                    dve.wait_ge(spread_turned, q)
                for t in range(NT):
                    for i in range(2):
                        ins = dve.tensor_scalar(spread[:, t, i::2, :], slot_no[:, 0:2 - i, :],
                                                rank_n[:, t, bass.ds(2 * q + i, 1)],
                                                gate_n[:, t, bass.ds(2 * q + i, 1)], ALU.is_equal, ALU.mult)
                ins.then_inc(spread_ready, 1)
                for i in range(2):
                    swiglu(2 * q + i)
                    dve.wait_ge(down_done, 2 * q + i + 1)
                    part = slice(CAP * (1 - i), CAP * (1 - i) + CAP)
                    dve.tensor_copy(ye[1][part, :], down_ps[part, :]).then_inc(ye2_ready, 1)

            pair(0, 0, starting=True)
            with dve.Fori(1, NE // 2) as q:
                pair(q, 2 * q)
            dve.wait_ge(flag_ready, 1)
            over = dve.value_load(most_i[0:1, 0:1], min_val=0, max_val=SEQ)
            with dve.If(over > CAP):
                with dve.Fori(1, ROUNDS) as r:
                    with dve.Fori(0, NE // 2) as m:
                        pair(r * (NE // 2) + m, 2 * m)

            for t in range(NT):
                for half in range(2):
                    dve.wait_ge(moe_done, 2 * t + half + 1)
                    add_residual(t, half, wide[:, 2 * t + half, :])
                    if (t, half) == (1, 0):
                        invert(NT)
                        dve.tensor_scalar(shift[:, :], mv[:, 0, 0:1], rstd[:, 0, :], -1.0, ALU.mult,
                                          ALU.mult).then_inc(scale_ready, 1)
                    moments(t, half)
                variance(t)
            dve.wait_ge(ln2_in, 2 * 16)
            center(1, slice(0, D))
            invert(NT + 1)
            for half in halves:
                scale(1, half)


INS = ["x", "w_in", "b_in", "sinks", "w_o_attn", "w_pool_mix", "pool_scale", "w_o_pool", "w_out", "ln1_g", "ln1_b",
       "w_router", "b_router", "w_gu", "b_gu", "w_down", "b_down", "ln2_g", "ln2_b"]


def kernel(**inputs):
    import numpy as np
    import concourse.bacc as bacc
    from concourse.bass_utils import run_bass_kernel_spmd

    nc = bacc.Bacc("TRN2", target_bir_lowering=False, num_devices=1)
    arrays, args = {}, []
    for name in INS:
        a = np.ascontiguousarray(inputs[name])
        arrays[f"in_{name}_dram"] = a
        args.append(nc.dram_tensor(f"in_{name}_dram", a.shape, mybir.dt.from_np(a.dtype), kind="ExternalInput").ap())
    args.append(nc.dram_tensor("out_dram", (1, SEQ, D), F32, kind="ExternalOutput").ap())
    build_layer(nc, *args)
    r = run_bass_kernel_spmd(nc, [arrays], core_ids=[0])
    return r.results[0]["out_dram"]
```
